# Optimizing a Trainium2 kernel written in Bass

```python
import math
import jax, jax.numpy as jnp
from jax import lax
import numpy as np

D_MODEL = 1024
BATCH = 1
SEQ = 256
DEPTH = 1

CHUNK = 64
EPS = 1e-6

SSD_D_INNER = D_MODEL
SSD_HEAD_DIM = 64
SSD_HEADS = SSD_D_INNER // SSD_HEAD_DIM
SSD_GROUPS = 2
SSD_HEADS_PER_GROUP = SSD_HEADS // SSD_GROUPS
SSD_STATE = 128
SSD_CONV = 4
SSD_CONV_DIM = SSD_D_INNER + 2 * SSD_GROUPS * SSD_STATE

MLA_HEADS = 8
MLA_Q_RANK = 384
MLA_KV_RANK = 256
MLA_NOPE = 128
MLA_ROPE = 64
MLA_QK_DIM = MLA_NOPE + MLA_ROPE
MLA_V = 128
ROPE_BASE = 10000.0
Q_BLOCK = 128

N_EXPERTS = 32
TOP_K = 4
EXPERT_FF = D_MODEL
SWIGLU_ALPHA = 1.702
SWIGLU_LIMIT = 7.0
MOE_BLOCK = 128

N_BRANCHES = 2
OFF_XBC = SSD_D_INNER
OFF_DT = OFF_XBC + SSD_CONV_DIM
OFF_QLAT = OFF_DT + SSD_HEADS
OFF_KVLAT = OFF_QLAT + MLA_Q_RANK
OFF_KROPE = OFF_KVLAT + MLA_KV_RANK
OFF_GATE = OFF_KROPE + MLA_ROPE
IN_DIM = OFF_GATE + N_BRANCHES * D_MODEL

kernel_name = 'hybrid_ssd_mla_moe_block'

def rms_norm(x, gain):
    xf = x.astype(jnp.float32)
    y = xf * lax.rsqrt(jnp.mean(xf * xf, axis=-1, keepdims=True) + EPS)
    return y.astype(x.dtype) * gain

def rope_tables(seq):
    pos = jnp.arange(seq, dtype=jnp.float32)
    inv = ROPE_BASE ** (-jnp.arange(0, MLA_ROPE, 2, dtype=jnp.float32) / MLA_ROPE)
    ang = pos[:, None] * inv[None, :]
    return jnp.cos(ang), jnp.sin(ang)

def apply_rope(x, cos, sin):
    half = MLA_ROPE // 2
    x1, x2 = x[..., :half], x[..., half:]
    c = cos[None, :, None, :].astype(x.dtype)
    s = sin[None, :, None, :].astype(x.dtype)
    return jnp.concatenate([x1 * c - x2 * s, x2 * c + x1 * s], axis=-1)

def ssd_scan(x, dt, a, bm, cm):
    b, s = x.shape[0], x.shape[1]
    nc = s // CHUNK
    xc = x.reshape(b, nc, CHUNK, SSD_GROUPS, SSD_HEADS_PER_GROUP, SSD_HEAD_DIM)
    dtc = dt.reshape(b, nc, CHUNK, SSD_GROUPS, SSD_HEADS_PER_GROUP)
    xdt = xc * dtc[..., None]
    da = (dtc * a.reshape(SSD_GROUPS, SSD_HEADS_PER_GROUP)).transpose(0, 3, 4, 1, 2)
    bc = bm.reshape(b, nc, CHUNK, SSD_GROUPS, SSD_STATE)
    cc = cm.reshape(b, nc, CHUNK, SSD_GROUPS, SSD_STATE)
    a_cum = jnp.cumsum(da, axis=-1)
    seg = a_cum[..., :, None] - a_cum[..., None, :]
    tri = jnp.tril(jnp.ones((CHUNK, CHUNK), dtype=bool))
    lmat = jnp.exp(jnp.where(tri, seg, -jnp.inf))
    cb = jnp.einsum('bclgn,bcsgn->bgcls', cc, bc)
    y_diag = jnp.einsum('bgecls,bcsgep->bclgep', cb[:, :, None] * lmat, xdt)
    decay_states = jnp.exp(a_cum[..., -1:] - a_cum)
    states = jnp.einsum('bcsgn,bgecs,bcsgep->cbgepn', bc, decay_states, xdt)
    chunk_decay = jnp.moveaxis(jnp.exp(a_cum[..., -1]), -1, 0)

    def step(h, inp):
        st, dec = inp
        return dec[..., None, None] * h + st, h

    _, prev = lax.scan(step, jnp.zeros_like(states[0]), (states, chunk_decay))
    y_off = jnp.einsum('bclgn,cbgepn,bgecl->bclgep', cc, prev, jnp.exp(a_cum))
    return (y_diag + y_off).reshape(b, s, SSD_HEADS, SSD_HEAD_DIM)

def ssd_branch(z, xbc, dt_raw, conv_w, conv_b, dt_bias, a_log, d_skip, g_out):
    b, s, _ = xbc.shape
    xbc = lax.conv_general_dilated(
        xbc, conv_w[:, None, :].astype(xbc.dtype), window_strides=(1,),
        padding=[(SSD_CONV - 1, 0)], dimension_numbers=('NWC', 'WIO', 'NWC'),
        feature_group_count=SSD_CONV_DIM) + conv_b
    xbc = jax.nn.silu(xbc)
    xs = xbc[..., :SSD_D_INNER]
    bm = xbc[..., SSD_D_INNER:SSD_D_INNER + SSD_GROUPS * SSD_STATE]
    cm = xbc[..., SSD_D_INNER + SSD_GROUPS * SSD_STATE:]
    xh = xs.reshape(b, s, SSD_HEADS, SSD_HEAD_DIM).astype(jnp.float32)
    dt = jax.nn.softplus(dt_raw.astype(jnp.float32) + dt_bias.astype(jnp.float32))
    a = -jnp.exp(a_log.astype(jnp.float32))
    y = ssd_scan(xh, dt, a,
                 bm.reshape(b, s, SSD_GROUPS, SSD_STATE).astype(jnp.float32),
                 cm.reshape(b, s, SSD_GROUPS, SSD_STATE).astype(jnp.float32))
    y = y + d_skip.astype(jnp.float32)[:, None] * xh
    y = y.reshape(b, s, SSD_D_INNER).astype(z.dtype) * jax.nn.silu(z)
    y = rms_norm(y.reshape(b, s, SSD_GROUPS, SSD_D_INNER // SSD_GROUPS),
                 g_out.reshape(SSD_GROUPS, SSD_D_INNER // SSD_GROUPS))
    return y.reshape(b, s, SSD_D_INNER)

def mla_branch(q_lat, kv_lat, k_rope, g_q_lat, w_q_up, g_kv_lat, w_kv_up, g_qk_q, g_qk_k):
    b, s, _ = q_lat.shape
    q = (rms_norm(q_lat, g_q_lat) @ w_q_up).reshape(b, s, MLA_HEADS, MLA_QK_DIM)
    kv = (rms_norm(kv_lat, g_kv_lat) @ w_kv_up).reshape(b, s, MLA_HEADS, MLA_NOPE + MLA_V)
    k_nope, v = kv[..., :MLA_NOPE], kv[..., MLA_NOPE:]
    k = jnp.concatenate(
        [k_nope, jnp.broadcast_to(k_rope[:, :, None, :], (b, s, MLA_HEADS, MLA_ROPE))], axis=-1)
    q = rms_norm(q, g_qk_q)
    k = rms_norm(k, g_qk_k)
    cos, sin = rope_tables(s)
    q = jnp.concatenate([q[..., :MLA_NOPE], apply_rope(q[..., MLA_NOPE:], cos, sin)], axis=-1)
    k = jnp.concatenate([k[..., :MLA_NOPE], apply_rope(k[..., MLA_NOPE:], cos, sin)], axis=-1)
    q = q.transpose(0, 2, 1, 3)
    k = k.transpose(0, 2, 1, 3)
    v = v.transpose(0, 2, 1, 3)
    scale = MLA_QK_DIM ** -0.5
    chunk_id = jnp.arange(s) // CHUNK
    outs = []
    for j in range(s // Q_BLOCK):
        lo, hi = j * Q_BLOCK, (j + 1) * Q_BLOCK
        sc = jnp.einsum('bhqd,bhkd->bhqk', q[:, :, lo:hi], k[:, :, :hi]).astype(jnp.float32) * scale
        mask = chunk_id[:hi][None, :] <= chunk_id[lo:hi][:, None]
        p = jax.nn.softmax(jnp.where(mask, sc, -jnp.inf), axis=-1)
        outs.append(jnp.einsum('bhqk,bhkd->bhqd', p.astype(v.dtype), v[:, :, :hi]))
    o = jnp.concatenate(outs, axis=2)
    return o.transpose(0, 2, 1, 3).reshape(b, s, MLA_HEADS * MLA_V)

def moe(h, w_router, b_router, w_gate_up, b_gate_up, w_down, b_down):
    t, d = h.shape
    logits = (h @ w_router + b_router).astype(jnp.float32)
    top_vals, top_idx = lax.top_k(logits, TOP_K)
    gates = jax.nn.softmax(top_vals, axis=-1).astype(h.dtype)
    n_assign = t * TOP_K
    flat_e = top_idx.reshape(-1)
    order = jnp.argsort(flat_e)
    sorted_e = flat_e[order]
    tok = order // TOP_K
    gates_sorted = gates.reshape(-1)[order]
    counts = jnp.bincount(flat_e, length=N_EXPERTS)
    padded = ((counts + MOE_BLOCK - 1) // MOE_BLOCK) * MOE_BLOCK
    pad_end = jnp.cumsum(padded)
    pad_start = pad_end - padded
    start = jnp.cumsum(counts) - counts
    dest = pad_start[sorted_e] + (jnp.arange(n_assign) - start[sorted_e])
    n_blocks = -(-n_assign // MOE_BLOCK) + N_EXPERTS
    rows = n_blocks * MOE_BLOCK
    xs = jnp.zeros((rows, d), h.dtype).at[dest].set(h[tok])
    block_e = jnp.minimum(
        jnp.searchsorted(pad_end, jnp.arange(n_blocks) * MOE_BLOCK, side='right'), N_EXPERTS - 1)

    def expert_block(args):
        xb, e = args
        gu = xb @ w_gate_up[e] + b_gate_up[e]
        glu = jnp.minimum(gu[..., :EXPERT_FF], SWIGLU_LIMIT)
        lin = jnp.clip(gu[..., EXPERT_FF:], -SWIGLU_LIMIT, SWIGLU_LIMIT)
        act = glu * jax.nn.sigmoid(SWIGLU_ALPHA * glu) * (lin + 1.0)
        return act @ w_down[e] + b_down[e]

    ys = lax.map(expert_block, (xs.reshape(n_blocks, MOE_BLOCK, d), block_e)).reshape(rows, d)
    y_assign = ys[dest] * gates_sorted[:, None]
    return jax.ops.segment_sum(y_assign, tok, num_segments=t)

def setup_inputs(seed: int = 0) -> dict:
    key = jax.random.key(seed)
    ks = jax.random.split(key, 32)
    f32 = jnp.float32
    L = DEPTH

    def normal(k, shape, fan_in):
        return jax.random.normal(k, shape, f32) * fan_in ** -0.5

    def gain(k, shape):
        return 1.0 + 0.1 * jax.random.normal(k, shape, f32)

    def bias(k, shape):
        return 0.01 * jax.random.normal(k, shape, f32)

    dt0 = jnp.exp(jax.random.uniform(ks[5], (L, SSD_HEADS), f32, math.log(1e-3), math.log(1e-1)))
    return {
        'x': jax.random.normal(ks[0], (BATCH, SEQ, D_MODEL), f32),
        'g_mix': gain(ks[1], (L, D_MODEL)),
        'w_in': normal(ks[2], (L, D_MODEL, IN_DIM), D_MODEL),
        'conv_w': normal(ks[3], (L, SSD_CONV, SSD_CONV_DIM), SSD_CONV),
        'conv_b': bias(ks[4], (L, SSD_CONV_DIM)),
        'dt_bias': dt0 + jnp.log(-jnp.expm1(-dt0)),
        'a_log': jnp.log(jax.random.uniform(ks[6], (L, SSD_HEADS), f32, 1.0, 16.0)),
        'd_skip': gain(ks[7], (L, SSD_HEADS)),
        'g_ssd_out': gain(ks[8], (L, SSD_D_INNER)),
        'w_ssd_out': normal(ks[9], (L, SSD_D_INNER, D_MODEL), SSD_D_INNER),
        'g_q_lat': gain(ks[10], (L, MLA_Q_RANK)),
        'w_q_up': normal(ks[11], (L, MLA_Q_RANK, MLA_HEADS * MLA_QK_DIM), MLA_Q_RANK),
        'g_kv_lat': gain(ks[12], (L, MLA_KV_RANK)),
        'w_kv_up': normal(ks[13], (L, MLA_KV_RANK, MLA_HEADS * (MLA_NOPE + MLA_V)), MLA_KV_RANK),
        'g_qk_q': gain(ks[14], (L, MLA_QK_DIM)),
        'g_qk_k': gain(ks[15], (L, MLA_QK_DIM)),
        'w_mla_out': normal(ks[16], (L, MLA_HEADS * MLA_V, D_MODEL), MLA_HEADS * MLA_V),
        'w_o': normal(ks[17], (L, D_MODEL, D_MODEL), D_MODEL),
        'g_ffn': gain(ks[18], (L, D_MODEL)),
        'w_router': normal(ks[19], (L, D_MODEL, N_EXPERTS), D_MODEL),
        'b_router': bias(ks[20], (L, N_EXPERTS)),
        'w_gate_up': normal(ks[21], (L, N_EXPERTS, D_MODEL, 2 * EXPERT_FF), D_MODEL),
        'b_gate_up': bias(ks[22], (L, N_EXPERTS, 2 * EXPERT_FF)),
        'w_down': normal(ks[23], (L, N_EXPERTS, EXPERT_FF, D_MODEL), EXPERT_FF),
        'b_down': bias(ks[24], (L, N_EXPERTS, D_MODEL)),
    }

def reference(x, g_mix, w_in, conv_w, conv_b, dt_bias, a_log, d_skip, g_ssd_out, w_ssd_out,
              g_q_lat, w_q_up, g_kv_lat, w_kv_up, g_qk_q, g_qk_k, w_mla_out, w_o,
              g_ffn, w_router, b_router, w_gate_up, b_gate_up, w_down, b_down):
    b, s, d = x.shape
    for l in range(DEPTH):
        h = rms_norm(x, g_mix[l])
        proj = h @ w_in[l]
        z = proj[..., :OFF_XBC]
        xbc = proj[..., OFF_XBC:OFF_DT]
        dt_raw = proj[..., OFF_DT:OFF_QLAT]
        q_lat = proj[..., OFF_QLAT:OFF_KVLAT]
        kv_lat = proj[..., OFF_KVLAT:OFF_KROPE]
        k_rope = proj[..., OFF_KROPE:OFF_GATE]
        gate_logits = proj[..., OFF_GATE:]
        y_ssd = ssd_branch(z, xbc, dt_raw, conv_w[l], conv_b[l], dt_bias[l], a_log[l],
                           d_skip[l], g_ssd_out[l]) @ w_ssd_out[l]
        y_mla = mla_branch(q_lat, kv_lat, k_rope, g_q_lat[l], w_q_up[l], g_kv_lat[l],
                           w_kv_up[l], g_qk_q[l], g_qk_k[l]) @ w_mla_out[l]
        g = jax.nn.sigmoid(gate_logits.astype(jnp.float32)).astype(x.dtype)
        merged = g[..., :d] * y_ssd + g[..., d:] * y_mla
        x = x + merged @ w_o[l]
        h2 = rms_norm(x, g_ffn[l]).reshape(b * s, d)
        x = x + moe(h2, w_router[l], b_router[l], w_gate_up[l], b_gate_up[l],
                    w_down[l], b_down[l]).reshape(b, s, d)
    return x


_drawn_inputs = setup_inputs


def setup_inputs(seed=0):
    import zlib

    import numpy as np

    out = dict(_drawn_inputs(seed))
    spreads = {}
    factors = {'conv_b': 3.867, 'b_gate_up': 8.0, 'b_down': 8.0}
    for name, (base, spread) in spreads.items():
        noise = np.random.default_rng([zlib.crc32(name.encode()), seed]).standard_normal(out[name].shape)
        drawn = base * np.exp(spread * noise) if base else spread * noise
        out[name] = __import__('jax').numpy.asarray(drawn.astype(out[name].dtype))
    for name, factor in factors.items():
        out[name] = (out[name] * factor).astype(out[name].dtype)
    return out
```

```python
from contextlib import ExitStack

import numpy as np
import concourse.bass as bass
from concourse import mybir

F32 = mybir.dt.float32
F32R = mybir.dt.float32r
BF16 = mybir.dt.bfloat16
I32 = mybir.dt.int32
U32 = mybir.dt.uint32
ALU = mybir.AluOpType
ACT = mybir.ActivationFunctionType
AX = mybir.AxisListType

P = 128
D = 1024
TOKENS = 256
TT = TOKENS // P
KD = D // P
EPS = 1e-6

HEADS = 16
HD = 64
GROUPS = 2
HG = HEADS // GROUPS
STATE = 128
CONV = 4
XBC = D + 2 * GROUPS * STATE
XC = XBC // P
OFF_XBC = D
OFF_DT = OFF_XBC + XBC

AH = 8
QR, KVR = 384, 256
NOPE, ROPE, VD = 128, 64, 128
QK = NOPE + ROPE
OFF_Q = OFF_DT + HEADS
OFF_KV = OFF_Q + QR
OFF_KR = OFF_KV + KVR
OFF_GATE = OFF_KR + ROPE
CA = HEADS + QR
CB_ = KVR + ROPE
LAT = CA + CB_
SCALE = QK ** -0.5
CHUNK = 64

EXPERTS = 32
TOPK = 4
FF = D
CAP = 64
PASSES = TOKENS // CAP
ARENA = 32964
GE = 4
NG = EXPERTS // GE
ALPHA, LIMIT = 1.702, 7.0
NEG = -1e30

SLOT = 2048
RAW = 6
RING = 8
HIGHS = 4
EJ = 12
HALF = 4
POOL_PLACES = (2, 8)
DVE_PLACES = tuple(j for j in range(EJ) if j not in POOL_PLACES)
POOL_FIRST = sum(j in POOL_PLACES for j in range(6, 10))
DVE_FIRST = HALF - POOL_FIRST

FRONT_SLOTS = (
    [("w_in", k, 4, OFF_DT, CA, "lat1") for k in (0, 4)] + [("w_in", k, 4, OFF_KV, CB_, "lat3") for k in (0, 4)]
    + [("w_in", k, 4, OFF_XBC + 512 * s, 512, f"xbc{2 * s + 1}") for s in range(3) for k in (0, 4)]
    + [("w_in", k, 4, 512 * s, 512, f"z{2 * s + 1}") for s in range(2) for k in (0, 4)]
    + [("w_q_up", 0, 3, 512 * s, 512, f"qup{2 * s + 1}") for s in range(3)]
    + [("w_kv_up", 0, 2, 1024 * s, 1024, f"kvup{4 * s + 3}") for s in range(2)]
    + [("w_in", k, 4, OFF_GATE + 512 * s, 512, f"gate{2 * s + 1}") for s in range(4) for k in (0, 4)]
    + [("w_ssd_out", k, 4, 512 * s, 512, f"ssdout{2 * s + 1}") for s in range(2) for k in (0, 4)]
    + [("w_mla_out", k, 4, 512 * s, 512, f"mlaout{2 * s + 1}") for s in range(2) for k in (0, 4)]
    + [("w_o", k, 4, 512 * s, 512, f"wo{2 * s + 1}") for s in range(2) for k in (0, 4)])
NF = len(FRONT_SLOTS)

PRODUCTS = (
    [(f"hT{n}", "dve") for n in range(4)]
    + [(f"lat{n}", "act") for n in range(4)]
    + [(f"xbc{n}", "act") for n in range(6)]
    + [(f"z{n}", "act") for n in range(4)]
    + [(f"latT{n}", "dve") for n in range(4)]
    + [(f"qup{n}", "act") for n in range(6)]
    + [(f"kvup{n}", "act") for n in range(8)]
    + [(f"gate{n}", "act") for n in range(8)]
    + [(f"xsT{n}", "act") for n in range(4)]
    + [("btok", "dve"), ("cb", "dve"), ("acum", "dve")]
    + [(x, "act" if x[0] == "a" else "dve") for x in
       ("acumb0 acumb1 acumb2 acumb3 state0 state1 yoff0 yoff1 ydiag0 acumb4 acumb5 ydiag1 acumb6 acumb7 "
        "ydiag2 ydiag3".split())]
    + [(f"qT{n}", "act") for n in range(6)]
    + [(f"yT{n}", "dve") for n in range(4)]
    + [(f"ssdout{n}", "dve") for n in range(4)]
    + [(f"kT{n}", "act") for n in range(6)]
    + [(x, "act" if x[0] in "SP" else "dve") for x in
       ("S0 S1 S2 PT0 S3 PT1 O0 PT2 O1 S4 PT3 O2 S5 PT4 O3 PT5 O4 O5".split())]
    + [(f"mlaout{n}", "dve") for n in range(4)]
    + [(f"mT{n}", "act") for n in range(4)]
    + [(f"wo{n}", "dve") for n in range(4)]
    + [(f"h2T{n}", "act") for n in range(4)]
    + [("logits", "dve"), ("rank", "dve"), ("gatesT", "dve")]
    + [(f"bias{n}", "dve") for n in range(4)])
INDEX = {name: n for n, (name, _) in enumerate(PRODUCTS)}
ORDINAL = {name: sum(e == engine for _, e in PRODUCTS[:n]) for n, (name, engine) in enumerate(PRODUCTS)}
SCORES = [(0, 0, 4), (0, 1, 4), (1, 0, 2), (1, 1, 2), (1, 4, 2), (1, 5, 2)]


def build(nc, x, w_in, w_q_up, w_kv_up, w_ssd_out, w_mla_out, w_o, w_router, w_gate_up, w_down,
          g_mix, conv_w, conv_b, dt_bias, a_log, d_skip, g_ssd_out, g_q_lat, g_kv_lat, g_qk_q, g_qk_k,
          g_ffn, b_router, b_gate_up, b_down, cos, sin, out):
    weights = {"w_in": w_in, "w_q_up": w_q_up, "w_kv_up": w_kv_up, "w_ssd_out": w_ssd_out,
               "w_mla_out": w_mla_out, "w_o": w_o}
    with ExitStack() as ctx:
        def sb(name, shape, dt=F32, where=ctx):
            return where.enter_context(nc.sbuf_tensor(name, shape, dt))

        def sem(name):
            return ctx.enter_context(nc.semaphore(name))

        with ExitStack() as named:
            raw = sb("raw", [P, RAW, SLOT], where=named)
        low = sb("low", [P, RAW, SLOT], F32R)
        resid = sb("resid", [P, TT, D])
        gain_ffn = sb("gain_ffn", [P, D])
        bdown = sb("bdown", [EXPERTS, D])
        wrouter = sb("wrouter", [P, KD, EXPERTS])
        bgu = sb("bgu", [P, EXPERTS, 16])
        ident = sb("ident", [P, P])
        ones = sb("ones", [P, P])
        stacked = sb("stacked", [P, CAP])
        upper = sb("upper", [P, P])
        identb = sb("identb", [P, P], BF16)
        onesb = sb("onesb", [P, P], BF16)
        strictb = sb("strictb", [P, P], BF16)
        causal = sb("causal", [P, P], BF16)
        amask = sb("amask", [P, 2 * P], BF16)
        gmix = sb("gmix", [P, KD])
        cw = sb("cw", [P, XC, CONV])
        cbias = sb("cbias", [P, XC])
        gssd = sb("gssd", [P, KD])
        glat = sb("glat", [P, 5])
        vec16 = sb("vec16", [P, 3, HEADS])
        gq = sb("gq", [P, QK])
        gk = sb("gk", [P, QK])
        brouter = sb("brouter", [P, EXPERTS])
        trig = sb("trig", [P, 2, TT, ROPE // 2])
        stat = sb("stat", [P, 64])
        qkstat = sb("qkstat", [P, 2, TT, AH])
        krsum = sb("krsum", [P, TT])
        sp = sb("sp", [P, 8, TT, HEADS])
        nmax = sb("nmax", [P, 6, 4])
        psums = sb("psums", [P, 6, 4])
        iota_e = sb("iota_e", [P, EXPERTS])
        slot_no = sb("slot_no", [P, P])
        lg = sb("lg", [P, TT, EXPERTS])
        top = sb("top", [P, TT, 8])
        topi = sb("topi", [P, TT, 8], U32)
        topf = sb("topf", [P, TT, 8])
        tg = sb("tg", [P, TT, 8])
        onehot = sb("onehot", [P, TOPK, EXPERTS])
        picked = sb("picked", [P, TT, EXPERTS])
        pickedb = sb("pickedb", [P, TT, EXPERTS], BF16)
        gates = sb("gates", [P, TT, EXPERTS + GE])
        gatesT = sb("gatesT", [EXPERTS, TOKENS])
        pos = sb("pos", [P, TT, PASSES * EXPERTS + GE])
        load = sb("load", [P, 4])
        loadi = sb("loadi", [P, 2], I32)

        front = ExitStack()
        arena = sb("arena", [P, ARENA], F32, front)
        at = [0]

        def carve(n, start=None):
            a = at[0] if start is None else start
            if start is None:
                at[0] += n
            return arena[:, a:a + n], a

        hT_, hT_at = carve(2048)
        lat_, _ = carve(TT * LAT)
        xc_, xc_at = carve(XC * TOKENS)
        q_, _ = carve(TT * AH * QK)
        kv_, _ = carve(TT * AH * 256)
        gate_, _ = carve(TT * 2 * D)
        zs_, zs_at = carve(TT * D)
        cb_, _ = carve(4 * P)
        A_, A = carve(8228)
        lm_, lm_at = carve(2048)
        y_, y_at = carve(2048)
        btok, _ = carve(2 * P)
        assert at[0] <= ARENA
        hT = hT_.rearrange("p (k t) -> p k t", k=KD)
        yT, oT = hT, hT
        lat = lat_.rearrange("p (t n) -> p t n", t=TT)
        qr = lat[:, :, HEADS:HEADS + AH * ROPE]
        xc = xc_.rearrange("p (c t) -> p c t", c=XC)
        qb = q_.rearrange("p (t h n) -> p t h n", t=TT, h=AH)
        kv = kv_.rearrange("p (t h n) -> p t h n", t=TT, h=AH)
        gate = gate_.rearrange("p (t n) -> p t n", t=TT)
        zs = zs_.rearrange("p (t n) -> p t n", t=TT)
        mT = zs_.rearrange("p (k t) -> p k t", k=KD)
        cb = cb_.rearrange("p (n l) -> p n l", n=4)
        xn = carve(2048, A)[0].rearrange("p (t n) -> p t n", t=TT)
        PADW = TOKENS + CONV - 1
        xbcp = carve(XC * PADW, A + 2048)[0].rearrange("p (c t) -> p c t", c=XC)
        conv = carve(XC * TOKENS, A + 2048 + XC * PADW)[0].rearrange("p (c t) -> p c t", c=XC)
        latent_T = carve(1280, A)[0].rearrange("p (k t) -> p k t", k=5)
        xs = carve(2048, A)[0].rearrange("p (t n) -> p t n", t=TT)
        xdt = carve(2048, A + 2048)[0].rearrange("p (t n) -> p t n", t=TT)
        xdec = carve(1024, A + 4096)[0]
        prev = carve(1024, A + 5120)[0]
        yoff = carve(1024, A + 6144)[0]
        kr = carve(1024, A + 7168)[0].rearrange("p (t h n) -> p t h n", t=TT, h=AH)
        kT = carve(2048, A)[0].rearrange("p (h t) -> p h t", h=AH)
        krT = carve(1024, A + 2048)[0].rearrange("p (h t) -> p h t", h=AH // 2)
        prob = carve(1536, A + 4096)[0].rearrange("p (b n) -> p b n", b=3)
        probT = carve(1536, A + 5632)[0].rearrange("p (b n) -> p b n", b=3)
        qT = carve(2048, xc_at)[0].rearrange("p (h t) -> p h t", h=AH)
        qrT = carve(1024, xc_at + 2048)[0].rearrange("p (h t) -> p h t", h=AH // 2)
        lmat = carve(2048, lm_at)[0].rearrange("p (b h l) -> p b h l", b=4, h=4)
        rope_v = carve(2048, lm_at)[0].rearrange("p (s h n) -> p s h n", s=8, h=AH)
        dump = carve(2048, lm_at)[0].rearrange("p (n c) -> p n c", n=4)
        sq = carve(1536, y_at)[0]
        rope_g = carve(1024, y_at)[0].rearrange("p (s h n) -> p s h n", s=4, h=AH)
        y = y_.rearrange("p (t n) -> p t n", t=TT)
        front.close()

        whi = sb("whi", [P, HIGHS, SLOT], F32R)
        with ExitStack() as named:
            raw_more = sb("raw_more", [P, RING - RAW, SLOT], where=named)
        low_more = sb("low_more", [P, RING - RAW, SLOT], F32R)
        gusb = sb("gusb", [P, 2, D])
        ysb = sb("ysb", [P, 2, D])
        h2hi = sb("h2hi", [P, TT, D], F32R)
        h2lo = sb("h2lo", [P, TT, D], F32R)
        xT = sb("xT", [P, KD, GE, P], F32R)
        actT = sb("actT", [P, KD, P], F32R)
        gu = sb("gu", [P, 8, CAP])
        sg = sb("sg", [P, 4, CAP])
        lin = sb("lin", [P, 4, CAP])
        af = sb("af", [P, 4, CAP])
        pick = sb("pick", [P, TT, GE * CAP], F32R)
        give = sb("give", [P, GE, TT, P])
        giveT = sb("giveT", [P, GE, TOKENS])
        posl = sb("posl", [P, TT, GE])
        gatel = sb("gatel", [P, TT, GE])
        h2 = gusb
        h2T = ysb[:, :, :].rearrange("p a (k t) -> p (a k) t", t=TOKENS)

        ps = [ctx.enter_context(nc.psum_tensor(f"bank{n}", [P, 512], F32)) for n in range(2)]
        ps2 = ctx.enter_context(nc.psum_tensor("bank23", [P, 2, 512], F32))
        psy = ctx.enter_context(nc.psum_tensor("bank45", [P, 2, 512], F32))
        pst = ctx.enter_context(nc.psum_tensor("bank6", [P, 512], F32))
        psm = ctx.enter_context(nc.psum_tensor("bank7", [P, 512], F32))
        banks = [ps[0][:, :], ps[1][:, :], ps2[:, 0, :], ps2[:, 1, :], psy[:, 0, :], psy[:, 1, :],
                 pst[:, :], psm[:, :]]

        def bank(name):
            return banks[INDEX[name] % 8]

        x_in = sem("x_in")
        small_in = sem("small_in")
        late_in = sem("late_in")
        raw_in = [sem(f"raw_in{r}") for r in range(RING)]
        filled = sem("filled")
        emptied = {"act": sem("emptied_act"), "dve": sem("emptied_dve")}
        consts = sem("consts")
        dve_step = sem("dve_step")
        act_step = sem("act_step")
        pool_step = sem("pool_step")
        x_sq = sem("x_sq")
        x_ms = sem("x_ms")
        x_rt = sem("x_rt")
        xn_done = sem("xn_done")
        lat_sq = sem("lat_sq")
        lat_ms = sem("lat_ms")
        lat_rt = sem("lat_rt")
        lat_done = sem("lat_done")
        dt_raw = sem("dt_raw")
        dt_exp = sem("dt_exp")
        dt_one = sem("dt_one")
        dt_ln = sem("dt_ln")
        dt_done = sem("dt_done")
        padded = sem("padded")
        conv_done = sem("conv_done")
        silu_done = sem("silu_done")
        sq_ready = sem("sq_ready")
        sq_read = sem("sq_read")
        qk_ms = sem("qk_ms")
        qk_rt = sem("qk_rt")
        qk_inv = sem("qk_inv")
        q_done = sem("q_done")
        k_done = sem("k_done")
        decay_done = sem("decay_done")
        xdt_done = sem("xdt_done")
        mmat_done = sem("mmat_done")
        prev_done = sem("prev_done")
        xskip_done = sem("xskip_done")
        yz_done = sem("yz_done")
        y_sq = sem("y_sq")
        y_ms = sem("y_ms")
        y_rt = sem("y_rt")
        yn_done = sem("yn_done")
        max_done = sem("max_done")
        prob_done = sem("prob_done")
        merged = sem("merged")
        x2_sq = sem("x2_sq")
        x2_ms = sem("x2_ms")
        x2_rt = sem("x2_rt")
        h2_done = sem("h2_done")
        h2_split = sem("h2_split")
        top_done = sem("top_done")
        top_exp = sem("top_exp")
        picked_done = sem("picked_done")
        gates_done = sem("gates_done")
        routed = sem("routed")
        w_free = sem("w_free")
        lo_done = sem("lo_done_dve")
        lo_done_pool = sem("lo_done_pool")
        hi_done = sem("hi_done")
        gu_out = sem("gu_out")
        t_filled = sem("t_filled")
        t_read = sem("t_read")
        glu_done = sem("glu_done")
        sig_done = sem("sig_done")
        lin_done = sem("lin_done")
        prod_done = sem("prod_done")
        af_done = sem("af_done")
        ahi_done = sem("ahi_done")
        act_ready = sem("act_ready")
        y_out = sem("y_out")
        sc_filled = sem("sc_filled")
        y_added = sem("y_added")
        pick_ready = sem("pick_ready")
        give_ready = sem("give_ready")
        g_filled = sem("g_filled")
        g_out = sem("g_out")
        x_filled = sem("x_filled")
        x_out = sem("x_out")
        posl_done = sem("posl_done")
        zeroed = sem("zeroed")
        stored = sem("stored")

        def product(eng, name):
            eng.wait_ge(filled, INDEX[name] + 1)
            return bank(name)

        def raw_in_count(n):
            return 16 * (n // RAW + 1)

        def front_slot(n):
            _, _, kk, _, cols, _ = FRONT_SLOTS[n]
            return raw[:, n % RAW, 0:kk * cols].rearrange("p (k n) -> p k n", k=kk)

        def nth(i, j):
            return HALF + EJ * i + j if i >= 0 else j - 6

        def ring_slot(n):
            n %= RING
            return raw[:, n, :] if n < RAW else raw_more[:, n - RAW, :]

        def low_slot(n):
            n %= RING
            return low[:, n, :] if n < RAW else low_more[:, n - RAW, :]

        def high_slot(n):
            return whi[:, n % HIGHS, :]

        def low_order(places, first, G, i, j):
            if i < 0:
                return sum(p in places for p in range(6, j + 1))
            return G * (GE * len(places)) + first + len(places) * i + places.index(j) + 1

        block = ctx.enter_context(nc.Block())

        @block.sync
        def _(sp_):
            sp_.dma_start(resid[:, :, :], x.rearrange("(t p) d -> p t d", p=P)).then_inc(x_in, 16)
            for n, (name, k0, kk, c0, cols, _) in enumerate(FRONT_SLOTS):
                if n >= RAW:
                    sp_.wait_ge(filled, INDEX[FRONT_SLOTS[n - RAW][5]] + 1)
                src = weights[name].rearrange("(k p) n -> p k n", p=P)[:, k0:k0 + kk, c0:c0 + cols]
                sp_.dma_start(front_slot(n), src).then_inc(raw_in[n % RAW], 16)

            def load_slot(e, n):
                i, j = (n - HALF) // EJ, (n - HALF) % EJ
                if n < HALF:
                    src = w_gate_up[e, n]
                elif i == GE - 1 and j in range(6, 10):
                    src = w_gate_up[next_of(e), j - 6]
                elif j < 4:
                    src = w_gate_up[e + i, HALF + j]
                elif 6 <= j < 10:
                    src = w_gate_up[e + i + 1, j - 6]
                else:
                    src = w_down[e + i, j - 4 if j < 6 else j - 8]
                sp_.dma_start(ring_slot(n), src).then_inc(raw_in[n % RING], 16)

            def next_of(e):
                return 0 if isinstance(e, int) and e == EXPERTS - GE else e + GE

            def rest_of_group(G, e):
                for n in range(RING, HALF + GE * EJ):
                    sp_.wait_ge(w_free, G * (GE * EJ) + n + 1)
                    load_slot(e, n)

            def start_of_group(G, e):
                for n in range(HALF, RING):
                    sp_.wait_ge(w_free, G * (GE * EJ) + n + 1)
                    load_slot(e, n)

            sp_.wait_ge(filled, INDEX["wo3"] + 1)
            for n in range(RING):
                load_slot(0, n)
            sp_.wait_ge(routed, 1)
            load_max = sp_.value_load(loadi[0:1, 0:1], min_val=0, max_val=TOKENS)
            runs = sp_.value_load(loadi[0:1, 1:2], min_val=0, max_val=PASSES * EXPERTS)
            with sp_.Fori(0, PASSES) as b:
                with sp_.If(load_max > b * CAP):
                    with sp_.Fori(0, NG - 1) as g:
                        rest_of_group(b * NG + g, g * GE)
                        start_of_group(b * NG + g + 1, g * GE + GE)
                    rest_of_group(b * NG + NG - 1, EXPERTS - GE)
                    with sp_.If(load_max > b * CAP + CAP):
                        start_of_group(b * NG + NG, 0)
            sp_.wait_ge(y_added, runs * 2 + 4)
            sp_.dma_start(out.rearrange("(t p) d -> p t d", p=P), resid[:, :, :]).then_inc(stored, 16)
            sp_.wait_ge(stored, 16)

        @block.gpsimd
        def _(pool):
            steps = [0]

            def settle(ins):
                steps[0] += 1
                ins.then_inc(pool_step, 1)
                pool.wait_ge(pool_step, steps[0])

            for t_, v in ((ident, 0.0), (ones, 1.0), (stacked, 0.0), (upper, 1.0), (identb, 0.0),
                          (onesb, 1.0), (strictb, 1.0), (causal, 0.0), (amask, 0.0)):
                settle(pool.memset(t_[:, :], v))
            diag = [[-1, P]]
            settle(pool.affine_select(out=ident[:, :], in_=ident[:, :], compare_op=ALU.not_equal, fill=1.0,
                                      base=0, pattern=diag, channel_multiplier=1))
            settle(pool.affine_select(out=identb[:, :], in_=identb[:, :], compare_op=ALU.not_equal, fill=1.0,
                                      base=0, pattern=diag, channel_multiplier=1))
            for base in (0, -CAP):
                settle(pool.affine_select(out=stacked[:, :], in_=stacked[:, :], compare_op=ALU.not_equal,
                                          fill=1.0, base=base, pattern=[[-1, CAP]], channel_multiplier=1))
            settle(pool.affine_select(out=upper[:, :], in_=upper[:, :], compare_op=ALU.is_ge, fill=0.0,
                                      base=0, pattern=[[1, P]], channel_multiplier=-1))
            settle(pool.affine_select(out=strictb[:, :], in_=strictb[:, :], compare_op=ALU.is_gt, fill=0.0,
                                      base=0, pattern=[[1, P]], channel_multiplier=-1))
            settle(pool.affine_select(out=causal[:, :], in_=causal[:, :], compare_op=ALU.is_ge, fill=NEG,
                                      base=0, pattern=[[1, P]], channel_multiplier=-1))
            settle(pool.affine_select(out=amask[:, P + CHUNK:2 * P], in_=amask[:, P + CHUNK:2 * P], compare_op=ALU.is_ge,
                                      fill=NEG, base=-CHUNK, pattern=[[0, P - CHUNK]], channel_multiplier=1))
            settle(pool.iota(iota_e[:, :], pattern=[[1, EXPERTS]], base=0, channel_multiplier=0,
                             allow_small_or_imprecise_dtypes=True))
            pool.iota(slot_no[:, :].rearrange("p (a n) -> p a n", a=2), pattern=[[0, 2], [1, CAP]], base=0,
                      channel_multiplier=0, allow_small_or_imprecise_dtypes=True).then_inc(consts, 1)
            pool.memset(xbcp[:, :, 0:CONV - 1], 0.0).then_inc(padded, 1)

            n = 0
            for t in range(TT):
                pool.wait_ge(emptied["act"], ORDINAL["qup5"] + 1)
                if n:
                    pool.wait_ge(sq_read, n)
                pool.tensor_tensor(sq[:, 0:AH * QK].rearrange("p (h n) -> p h n", h=AH), qb[:, t], qb[:, t],
                                   ALU.mult).then_inc(sq_ready, 1)
                n += 1
            for t in range(TT):
                pool.wait_ge(emptied["act"], ORDINAL["kvup7"] + 1)
                pool.wait_ge(sq_read, n)
                pool.tensor_tensor(sq[:, 0:AH * NOPE].rearrange("p (h n) -> p h n", h=AH),
                                   kv[:, t, :, 0:NOPE], kv[:, t, :, 0:NOPE], ALU.mult).then_inc(sq_ready, 1)
                n += 1
            pool.wait_ge(sq_read, n)
            pool.wait_ge(qk_inv, 1)
            pool.wait_ge(silu_done, 3)
            for t in range(TT):
                inv = qkstat[:, 1, t, :]
                kn = kv[:, t, :, 0:NOPE]
                settle(pool.tensor_tensor(kn, kn, inv.unsqueeze(2).to_broadcast([P, AH, NOPE]), ALU.mult))
                settle(pool.tensor_tensor(kn, kn, gk[:, 0:NOPE].unsqueeze(1).to_broadcast([P, AH, NOPE]), ALU.mult))
                krow = lat[:, t, LAT - ROPE:LAT].unsqueeze(1).to_broadcast([P, AH, ROPE])
                settle(pool.tensor_tensor(kr[:, t], krow, inv.unsqueeze(2).to_broadcast([P, AH, ROPE]), ALU.mult))
                settle(pool.tensor_tensor(kr[:, t], kr[:, t], gk[:, NOPE:QK].unsqueeze(1).to_broadcast([P, AH, ROPE]), ALU.mult))
                c = trig[:, 0, t, :].unsqueeze(1).to_broadcast([P, AH, ROPE // 2])
                s = trig[:, 1, t, :].unsqueeze(1).to_broadcast([P, AH, ROPE // 2])
                k1, k2 = kr[:, t, :, 0:ROPE // 2], kr[:, t, :, ROPE // 2:ROPE]
                pool.tensor_tensor(rope_g[:, 0], k1, c, ALU.mult)
                pool.tensor_tensor(rope_g[:, 1], k2, s, ALU.mult)
                pool.tensor_tensor(rope_g[:, 2], k2, c, ALU.mult)
                settle(pool.tensor_tensor(rope_g[:, 3], k1, s, ALU.mult))
                settle(pool.tensor_tensor(k1, rope_g[:, 0], rope_g[:, 1], ALU.subtract))
                ins = pool.tensor_tensor(k2, rope_g[:, 2], rope_g[:, 3], ALU.add)
                ins.then_inc(k_done, 1)
                pool.wait_ge(k_done, t + 1)
            pool.wait_ge(emptied["act"], ORDINAL["xsT3"] + 1)
            pool.wait_ge(dt_done, 1)
            for t in range(TT):
                xh = xs[:, t, :].rearrange("p (h n) -> p h n", h=HEADS)
                settle(pool.tensor_tensor(xdt[:, t, :].rearrange("p (h n) -> p h n", h=HEADS), xh,
                                          sp[:, 0, t, :].unsqueeze(2).to_broadcast([P, HEADS, HD]), ALU.mult))
            pool.wait_ge(decay_done, 2)
            pool.tensor_tensor(xdec.rearrange("p (h n) -> p h n", h=HEADS),
                               xdt[:, 0, :].rearrange("p (h n) -> p h n", h=HEADS),
                               sp[:, 3, 0, :].unsqueeze(2).to_broadcast([P, HEADS, HD]), ALU.mult).then_inc(xdt_done, 1)
            for t in range(TT):
                xh = xs[:, t, :].rearrange("p (h n) -> p h n", h=HEADS)
                pool.tensor_tensor(xh, xh, vec16[:, 2, :].unsqueeze(2).to_broadcast([P, HEADS, HD]),
                                   ALU.mult).then_inc(xskip_done, 1)

            def localise(column, column_g):
                pool.tensor_copy(posl[:, :, :], pos[:, :, column:column + GE] if isinstance(column, int)
                                 else pos[:, :, bass.ds(column, GE)])
                pool.tensor_copy(gatel[:, :, :], gates[:, :, column_g:column_g + GE] if isinstance(column_g, int)
                                 else gates[:, :, bass.ds(column_g, GE)]).then_inc(posl_done, 1)

            def pick_tokens():
                for t in range(TT):
                    for i in range(GE):
                        ins = pool.tensor_scalar(pick[:, t, CAP * i:CAP * i + CAP], slot_no[:, 0:CAP],
                                                 posl[:, t, i:i + 1], None, ALU.is_equal)
                ins.then_inc(pick_ready, 1)

            def give_gates(i):
                for t in range(TT):
                    ins = pool.tensor_scalar(give[:, i, t, :], slot_no[:, :], posl[:, t, i:i + 1],
                                             gatel[:, t, i:i + 1], ALU.is_equal, ALU.mult)
                ins.then_inc(give_ready, 1)

            def low_part(G, i, j):
                n = nth(i, j)
                pool.wait_ge(hi_done, G * (GE * EJ) + n + 1)
                pool.tensor_tensor(low_slot(n), ring_slot(n), high_slot(n).bitcast(F32),
                                   ALU.subtract).then_inc(lo_done_pool, 1)

            pool.wait_ge(w_free, RING)
            for j in POOL_PLACES:
                if j in range(6, 10):
                    low_part(0, -1, j)
            pool.wait_ge(filled, INDEX["logits"] + 1)
            pool.memset(ysb[:, :, :], 0.0).then_inc(zeroed, 1)
            pool.wait_ge(routed, 1)
            load_max = pool.value_load(loadi[0:1, 0:1], min_val=0, max_val=TOKENS)
            localise(0, 0)
            pool.wait_ge(posl_done, 1)
            for i in range(GE):
                give_gates(i)

            with pool.Fori(0, PASSES) as b:
                with pool.If(load_max > b * CAP):
                    with pool.Fori(0, NG) as g:
                        G = b * NG + g
                        for i in range(GE):
                            if i == 0:
                                pool.wait_ge(x_filled, G * KD + KD)
                                pool.wait_ge(give_ready, G * GE + GE)
                            low_part(G, i, POOL_PLACES[0])
                            if i == 0:
                                localise(G * GE + GE, g * GE + GE)
                                pool.wait_ge(posl_done, G + 2)
                            pool.wait_ge(g_filled, G * GE + i + 1)
                            low_part(G, i, POOL_PLACES[1])
                            if i == 0:
                                pick_tokens()
                            give_gates(i)

        @block.scalar
        def _(act):
            steps = [0]

            def settle(ins):
                steps[0] += 1
                ins.then_inc(act_step, 1)
                act.wait_ge(act_step, steps[0])

            for dst, src in ((gmix[:, :], g_mix), (vec16[:, 0, :], dt_bias), (vec16[:, 1, :], a_log),
                             (vec16[:, 2, :], d_skip), (glat[:, 0:3], g_q_lat), (glat[:, 3:5], g_kv_lat),
                             (cw[:, :, :], conv_w), (cbias[:, :], conv_b), (gssd[:, :], g_ssd_out),
                             (gq[:, :], g_qk_q), (gk[:, :], g_qk_k), (trig[:, 0, :, :], cos),
                             (trig[:, 1, :, :], sin)):
                act.dma_start(dst, src).then_inc(small_in, 16)
            for dst, src in ((gain_ffn[:, :], g_ffn), (bdown[:, :], b_down), (wrouter[:, :, :], w_router),
                             (bgu[:, :, :], b_gate_up), (brouter[:, :], b_router)):
                act.dma_start(dst, src).then_inc(late_in, 16)

            act.wait_ge(x_in, 16)
            for t in range(TT):
                act.activation(xn[:, t, :], resid[:, t, :], ACT.Square, accum_out=stat[:, t:t + 1]).then_inc(x_sq, 1)
            act.wait_ge(x_ms, 1)
            act.activation(stat[:, 2:4], stat[:, 2:4], ACT.Sqrt).then_inc(x_rt, 1)

            for n in range(4):
                t, part = n % 2, n // 2
                src = product(act, f"lat{n}")
                a, cols = (0, CA) if part == 0 else (CA, CB_)
                act.activation(lat[:, t, a:a + cols], src[:, 0:cols], ACT.Copy).then_inc(emptied["act"], 1)
            act.wait_ge(emptied["act"], ORDINAL["lat3"] + 1)
            act.wait_ge(xn_done, TT)
            act.wait_ge(filled, INDEX["hT3"] + 1)
            for t in range(TT):
                act.activation(xn[:, t, 0:QR], lat[:, t, HEADS:CA], ACT.Square,
                               accum_out=stat[:, 4 + t:5 + t]).then_inc(lat_sq, 1)
                act.activation(xn[:, t, 512:512 + KVR], lat[:, t, CA:CA + KVR], ACT.Square,
                               accum_out=stat[:, 6 + t:7 + t]).then_inc(lat_sq, 1)
                act.activation(xn[:, t, 800:800 + ROPE], lat[:, t, LAT - ROPE:LAT], ACT.Square,
                               accum_out=krsum[:, t:t + 1]).then_inc(lat_sq, 1)
            act.wait_ge(lat_ms, 1)
            act.activation(stat[:, 8:12], stat[:, 8:12], ACT.Sqrt).then_inc(lat_rt, 1)
            act.wait_ge(dt_raw, 1)
            settle(act.activation(sp[:, 2, :, :], sp[:, 1, :, :], ACT.Abs))
            act.activation(sp[:, 2, :, :], sp[:, 2, :, :], ACT.Exp, scale=-1.0).then_inc(dt_exp, 1)
            act.wait_ge(small_in, 13 * 16)
            act.activation(vec16[:, 1, :], vec16[:, 1, :], ACT.Exp).then_inc(dt_exp, 1)
            act.wait_ge(dt_one, 1)
            act.activation(sp[:, 4, :, :], sp[:, 3, :, :], ACT.Ln).then_inc(dt_ln, 1)
            act.wait_ge(padded, 1)
            for n in range(6):
                src = product(act, f"xbc{n}").rearrange("p (c t) -> p c t", c=2)
                act.activation(xbcp[:, 2 * n:2 * n + 2, CONV - 1:PADW], src, ACT.Copy).then_inc(emptied["act"], 1)
            for n in range(4):
                t, s = n % 2, n // 2
                act.activation(zs[:, t, 512 * s:512 * s + 512], product(act, f"z{n}"), ACT.Silu).then_inc(emptied["act"], 1)
            for n in range(3):
                act.wait_ge(conv_done, 4 * n + 4)
                act.activation(xc[:, 4 * n:4 * n + 4, :], conv[:, 4 * n:4 * n + 4, :], ACT.Silu).then_inc(silu_done, 1)
            for n in range(6):
                t, s = n % 2, n // 2
                act.activation(qb[:, t].rearrange("p h n -> p (h n)")[:, 512 * s:512 * s + 512],
                               product(act, f"qup{n}"), ACT.Copy).then_inc(emptied["act"], 1)
            for n in range(8):
                t, s = n % 2, n // 2
                act.activation(kv[:, t].rearrange("p h n -> p (h n)")[:, 512 * s:512 * s + 512],
                               product(act, f"kvup{n}"), ACT.Copy).then_inc(emptied["act"], 1)
            act.wait_ge(qk_ms, 1)
            act.activation(qkstat[:, :, :, :], qkstat[:, :, :, :], ACT.Sqrt).then_inc(qk_rt, 1)
            for n in range(8):
                t, s = n % 2, n // 2
                act.activation(gate[:, t, 512 * s:512 * s + 512], product(act, f"gate{n}"), ACT.Sigmoid).then_inc(emptied["act"], 1)
            act.wait_ge(silu_done, 3)
            for n in range(4):
                t, h = n % 2, n // 2
                act.activation(xs[:, t, 512 * h:512 * h + 512], product(act, f"xsT{n}"), ACT.Copy).then_inc(emptied["act"], 1)
            act.wait_ge(emptied["dve"], ORDINAL["acum"] + 1)
            act.activation(sp[:, 3, 0, :], sp[:, 7, 0, :], ACT.Exp).then_inc(decay_done, 1)
            act.activation(sp[:, 3, 1, :], sp[:, 6, 1, :], ACT.Exp, scale=-1.0).then_inc(decay_done, 1)
            for n in range(8):
                t = n // 4
                src = product(act, f"acumb{n}")
                if n >= 4:
                    act.wait_ge(filled, INDEX[f"ydiag{(n - 4) // 2}"] + 1)
                for hh in range(4):
                    h = 4 * (n % 4) + hh
                    ins = act.activation(lmat[:, n % 4, hh, :], src[:, P * hh:P * hh + P], ACT.Exp,
                                         bias=sp[:, 6, t, h:h + 1])
                    if hh == 3:
                        ins.then_inc(emptied["act"], 1)
            act.wait_ge(filled, INDEX["ydiag3"] + 1)
            for n in range(6):
                src = product(act, f"qT{n}").rearrange("p (h t) -> p h t", h=4)
                t, part = n % 2, n // 2
                dst = (qT[:, 4 * part:4 * part + 4, P * t:P * t + P] if part < 2 else
                       qrT[:, :, P * t:P * t + P])
                act.activation(dst, src, ACT.Copy).then_inc(emptied["act"], 1)
            act.wait_ge(yz_done, 2)
            for t in range(TT):
                for g in range(GROUPS):
                    act.activation(dump[:, 2 * t + g, :], y[:, t, 512 * g:512 * g + 512], ACT.Square,
                                   accum_out=stat[:, 12 + 2 * t + g:13 + 2 * t + g]).then_inc(y_sq, 1)
            act.wait_ge(y_ms, 1)
            act.activation(stat[:, 16:20], stat[:, 16:20], ACT.Sqrt).then_inc(y_rt, 1)
            act.wait_ge(yn_done, 4)
            for n in range(6):
                src = product(act, f"kT{n}").rearrange("p (h t) -> p h t", h=4)
                t, part = n % 2, n // 2
                dst = (kT[:, 4 * part:4 * part + 4, P * t:P * t + P] if part < 2 else
                       krT[:, :, P * t:P * t + P])
                act.activation(dst, src, ACT.Copy).then_inc(emptied["act"], 1)

            def softmax_exp(n):
                j, _, hs = SCORES[n]
                keys = P * (j + 1)
                src = product(act, f"S{n}")
                act.wait_ge(max_done, n + 1)
                if n >= 3:
                    act.wait_ge(filled, INDEX[f"PT{n - 3}"] + 1)
                for h in range(hs):
                    ins = act.activation(prob[:, n % 3, keys * h:keys * h + keys], src[:, keys * h:keys * h + keys],
                                         ACT.Exp, bias=nmax[:, n, h:h + 1], scale=SCALE,
                                         accum_out=psums[:, n, h:h + 1])
                ins.then_inc(emptied["act"], 1)

            def probs_by_key(n):
                src = product(act, f"PT{n}")
                if n >= 3:
                    act.wait_ge(filled, INDEX[f"O{n - 3}"] + 1)
                act.activation(probT[:, n % 3, :], src, ACT.Copy).then_inc(emptied["act"], 1)

            for name, who in PRODUCTS[INDEX["S0"]:INDEX["O5"] + 1]:
                if who == "act":
                    (softmax_exp if name[0] == "S" else probs_by_key)(int(name[-1]))
            for n in range(4):
                t, h = n % 2, n // 2
                src = product(act, f"mT{n}").rearrange("p (k t) -> p k t", k=4)
                act.activation(mT[:, 4 * h:4 * h + 4, P * t:P * t + P], src, ACT.Copy).then_inc(emptied["act"], 1)
            def gathered(k, G, gather_bank=psm):
                act.wait_ge(x_filled, G * KD + k + 1)
                src = gather_bank[:, :].rearrange("p (part i s) -> p part i s", part=2, i=GE)
                dst = xT[:, k, :, :].rearrange("p i (part s) -> p part i s", part=2)
                for part in range(2):
                    ins = act.activation(dst[:, part], src[:, part], ACT.Copy)
                ins.then_inc(x_out, 1)

            def high_part(G, i, j):
                n = nth(i, j)
                before = sum(1 for m in range(NF) if m % RAW == n % RING)
                act.wait_ge(raw_in[n % RING], G * (GE * EJ // RING * 16) + 16 * (before + n // RING + 1))
                act.wait_ge(w_free, G * (GE * EJ) + n + RING - HIGHS + 1)
                act.activation(high_slot(n), ring_slot(n), ACT.Copy).then_inc(hi_done, 1)

            def sums_out(G, i, hf):
                used = nth(i, 3) + 1 if hf else nth(i - 1, 9) + 1 if i else HALF
                act.wait_ge(w_free, G * (GE * EJ) + used + RING)
                for s in range(2):
                    src = ps[s][:, :] if hf == 0 else ps2[:, s, :]
                    act.activation(gusb[:, hf, 512 * s:512 * s + 512], src, ACT.Copy).then_inc(gu_out, 1)

            def sigmoid(G, i, hf):
                act.wait_ge(glu_done, G * (2 * GE) + 2 * i + hf + 1)
                act.activation(sg[:, :, :], gu[:, 0:4, :], ACT.Sigmoid, scale=ALPHA).then_inc(sig_done, 1)

            def outputs_out(E, i):
                act.wait_ge(w_free, E * EJ + HALF + RING)
                act.activation(ysb[:, (i - 1) % 2, :].rearrange("p (a n) -> p a n", a=2), psy[:, :, :],
                               ACT.Copy).then_inc(y_out, 1)

            for t in range(TT):
                act.wait_ge(emptied["dve"], ORDINAL["wo3"] + 1)
                act.activation(h2[:, t, :], resid[:, t, :], ACT.Square, accum_out=stat[:, 20 + t:21 + t]).then_inc(x2_sq, 1)
            act.wait_ge(x2_ms, 1)
            act.activation(stat[:, 22:24], stat[:, 22:24], ACT.Sqrt).then_inc(x2_rt, 1)
            for n in range(4):
                t, h = n % 2, n // 2
                src = product(act, f"h2T{n}").rearrange("p (k t) -> p k t", k=4)
                act.activation(h2T[:, 4 * h:4 * h + 4, P * t:P * t + P], src, ACT.Copy).then_inc(emptied["act"], 1)
            for j in range(6, 10):
                high_part(0, -1, j)
            act.wait_ge(top_done, 2)
            for t in range(TT):
                act.activation(tg[:, t, 0:4], top[:, t, 0:4], ACT.Exp, bias=tg[:, t, 4:5],
                               accum_out=tg[:, t, 5:6]).then_inc(top_exp, 1)

            for k in range(KD):
                gathered(k, 0, (psm, pst)[k % 2])
            act.wait_ge(routed, 1)
            load_max = act.value_load(loadi[0:1, 0:1], min_val=0, max_val=TOKENS)
            runs = act.value_load(loadi[0:1, 1:2], min_val=0, max_val=PASSES * EXPERTS)
            with act.Fori(0, PASSES) as b:
                with act.If(load_max > b * CAP):
                    with act.Fori(0, NG) as g:
                        G = b * NG + g
                        for i in range(GE):
                            E = G * GE + i
                            high_part(G, i, 0)
                            sums_out(G, i, 0)
                            for j in (1, 2, 3):
                                high_part(G, i, j)
                            act.wait_ge(g_filled, E + 1)
                            act.activation(giveT[:, i, :], psm[:, 0:TOKENS], ACT.Copy).then_inc(g_out, 1)
                            if i == GE - 1:
                                gathered(0, G + 1)
                            if i == 0:
                                act.wait_ge(zeroed, 3)
                            if i % 2 == 0:
                                outputs_out(E, i)
                            high_part(G, i, 4)
                            if i == GE - 1:
                                gathered(1, G + 1)
                                gathered(2, G + 1)
                            high_part(G, i, 5)
                            if i == GE - 1:
                                gathered(3, G + 1)
                            sigmoid(G, i, 0)
                            if i % 2:
                                act.wait_ge(sc_filled, 2 * E + 2)
                                outputs_out(E, i)
                            if i == GE - 1:
                                gathered(4, G + 1)
                            high_part(G, i, 6)
                            if i == GE - 1:
                                gathered(5, G + 1)
                                gathered(6, G + 1)
                            sums_out(G, i, 1)
                            high_part(G, i, 7)
                            if i == GE - 1:
                                gathered(7, G + 1)
                            for j in (8, 9, 10):
                                high_part(G, i, j)
                            sigmoid(G, i, 1)
                            high_part(G, i, 11)
            outputs_out(runs, 0)

        @block.vector
        def _(dve):
            steps = [0]

            def settle(ins):
                steps[0] += 1
                ins.then_inc(dve_step, 1)
                dve.wait_ge(dve_step, steps[0])

            def mean_eps(a, b, n, done):
                dve.tensor_scalar(stat[:, b], stat[:, a], 1.0 / n, EPS, ALU.mult, ALU.add).then_inc(done, 1)

            dve.wait_ge(x_sq, TT)
            mean_eps(slice(0, 2), slice(2, 4), D, x_ms)
            dve.wait_ge(x_rt, 1)
            settle(dve.reciprocal(stat[:, 2:4], stat[:, 2:4]))
            for t in range(TT):
                dve.tensor_scalar(xn[:, t, :], resid[:, t, :], stat[:, 2 + t:3 + t], None, ALU.mult).then_inc(xn_done, 1)
            dve.wait_ge(small_in, 13 * 16)
            for n in range(4):
                t, h = n % 2, n // 2
                src = product(dve, f"hT{n}").rearrange("p (k t) -> p k t", k=4)
                dve.tensor_tensor(hT[:, 4 * h:4 * h + 4, P * t:P * t + P], src,
                                  gmix[:, 4 * h:4 * h + 4].unsqueeze(2).to_broadcast([P, 4, P]),
                                  ALU.mult).then_inc(emptied["dve"], 1)
            dve.wait_ge(emptied["act"], ORDINAL["lat3"] + 1)
            dve.tensor_tensor(sp[:, 1, :, :], lat[:, :, 0:HEADS], vec16[:, 0, :].unsqueeze(1).to_broadcast([P, TT, HEADS]),
                              ALU.add).then_inc(dt_raw, 1)
            dve.wait_ge(lat_sq, 3 * TT)
            settle(dve.tensor_scalar(stat[:, 8:10], stat[:, 4:6], 1.0 / QR, EPS, ALU.mult, ALU.add))
            mean_eps(slice(6, 8), slice(10, 12), KVR, lat_ms)
            dve.wait_ge(lat_rt, 1)
            settle(dve.reciprocal(stat[:, 8:12], stat[:, 8:12]))
            for t in range(TT):
                dve.tensor_scalar(lat[:, t, HEADS:CA], lat[:, t, HEADS:CA], stat[:, 8 + t:9 + t], None, ALU.mult).then_inc(lat_done, 1)
                dve.tensor_scalar(lat[:, t, CA:CA + KVR], lat[:, t, CA:CA + KVR], stat[:, 10 + t:11 + t], None, ALU.mult).then_inc(lat_done, 1)
            dve.wait_ge(dt_exp, 2)
            e_, u_, l_, d_, s_ = (sp[:, n, :, :] for n in (2, 3, 4, 5, 6))
            dve.tensor_scalar(u_, e_, 1.0, None, ALU.add).then_inc(dt_one, 1)
            dve.wait_ge(dt_one, 1)
            settle(dve.tensor_scalar(d_, u_, -1.0, None, ALU.add))
            settle(dve.scalar_tensor_tensor(out=s_, in0=d_, scalar=0.0, in1=e_, op0=ALU.is_equal, op1=ALU.mult))
            settle(dve.tensor_scalar(d_, d_, 1e-30, None, ALU.max))
            settle(dve.reciprocal(d_, d_))
            settle(dve.tensor_tensor(d_, d_, e_, ALU.mult))
            dve.wait_ge(dt_ln, 1)
            settle(dve.tensor_tensor(d_, d_, l_, ALU.mult))
            settle(dve.tensor_tensor(d_, d_, s_, ALU.add))
            settle(dve.scalar_tensor_tensor(out=sp[:, 0, :, :], in0=sp[:, 1, :, :], scalar=0.0, in1=d_, op0=ALU.max, op1=ALU.add))
            dve.scalar_tensor_tensor(out=sp[:, 5, :, :], in0=sp[:, 0, :, :], scalar=-1.0,
                                     in1=vec16[:, 1, :].unsqueeze(1).to_broadcast([P, TT, HEADS]),
                                     op0=ALU.mult, op1=ALU.mult).then_inc(dt_done, 1)
            for c in range(XC):
                dve.wait_ge(emptied["act"], ORDINAL[f"xbc{c // 2}"] + 1)
                settle(dve.tensor_scalar(conv[:, c, :], xbcp[:, c, 0:TOKENS], cw[:, c, 0:1], cbias[:, c:c + 1], ALU.mult, ALU.add))
                for w in range(1, CONV):
                    ins = dve.scalar_tensor_tensor(out=conv[:, c, :], in0=xbcp[:, c, w:w + TOKENS], scalar=cw[:, c, w:w + 1],
                                                   in1=conv[:, c, :], op0=ALU.mult, op1=ALU.add)
                    if w < CONV - 1:
                        settle(ins)
                ins.then_inc(conv_done, 1)
            latT = latent_T
            for n in range(4):
                t, part = n % 2, n // 2
                k0, kk = (0, 3) if part == 0 else (3, 2)
                src = product(dve, f"latT{n}")[:, 0:kk * P].rearrange("p (k t) -> p k t", k=kk)
                dve.tensor_tensor(latT[:, k0:k0 + kk, P * t:P * t + P], src,
                                  glat[:, k0:k0 + kk].unsqueeze(2).to_broadcast([P, kk, P]),
                                  ALU.mult).then_inc(emptied["dve"], 1)
            for n in range(4):
                which, t = n // 2, n % 2
                width = QK if which == 0 else NOPE
                dve.wait_ge(sq_ready, n + 1)
                dve.tensor_reduce(qkstat[:, which, t, :], sq[:, 0:AH * width].rearrange("p (h n) -> p h n", h=AH),
                                  AX.X, ALU.add).then_inc(sq_read, 1)
            dve.wait_ge(sq_read, 4)
            settle(dve.tensor_tensor(qkstat[:, 1, :, :], qkstat[:, 1, :, :], krsum[:, :].unsqueeze(2).to_broadcast([P, TT, AH]), ALU.add))
            dve.tensor_scalar(qkstat[:, :, :, :], qkstat[:, :, :, :], 1.0 / QK, EPS, ALU.mult, ALU.add).then_inc(qk_ms, 1)
            dve.wait_ge(qk_rt, 1)
            dve.reciprocal(qkstat[:, :, :, :], qkstat[:, :, :, :]).then_inc(qk_inv, 1)
            dve.wait_ge(qk_inv, 1)
            for t in range(TT):
                settle(dve.tensor_tensor(qb[:, t], qb[:, t], qkstat[:, 0, t, :].unsqueeze(2).to_broadcast([P, AH, QK]), ALU.mult))
                settle(dve.tensor_tensor(qb[:, t], qb[:, t], gq[:, :].unsqueeze(1).to_broadcast([P, AH, QK]), ALU.mult))
                c = trig[:, 0, t, :].unsqueeze(1).to_broadcast([P, AH, ROPE // 2])
                s = trig[:, 1, t, :].unsqueeze(1).to_broadcast([P, AH, ROPE // 2])
                q1, q2 = qb[:, t, :, NOPE:NOPE + ROPE // 2], qb[:, t, :, NOPE + ROPE // 2:QK]
                r0 = 4 * t
                dve.tensor_tensor(rope_v[:, r0], q1, c, ALU.mult)
                dve.tensor_tensor(rope_v[:, r0 + 1], q2, s, ALU.mult)
                dve.tensor_tensor(rope_v[:, r0 + 2], q2, c, ALU.mult)
                settle(dve.tensor_tensor(rope_v[:, r0 + 3], q1, s, ALU.mult))
                rot = qr[:, t, :].rearrange("p (h n) -> p h n", h=AH)
                dve.tensor_tensor(rot[:, :, 0:ROPE // 2], rope_v[:, r0], rope_v[:, r0 + 1], ALU.subtract)
                dve.tensor_tensor(rot[:, :, ROPE // 2:ROPE], rope_v[:, r0 + 2], rope_v[:, r0 + 3], ALU.add).then_inc(q_done, 1)
            dve.tensor_copy(btok, product(dve, "btok")[:, 0:2 * P]).then_inc(emptied["dve"], 1)
            dve.tensor_copy(cb_, product(dve, "cb")).then_inc(emptied["dve"], 1)
            src = product(dve, "acum")
            cum = src[:, 0:2 * HEADS].rearrange("p (t h) -> p t h", t=TT)
            settle(dve.tensor_scalar(sp[:, 6, :, :], cum, -1.0, None, ALU.mult))
            dve.tensor_tensor(sp[:, 7, 0, :], src[:, 2 * HEADS:3 * HEADS], sp[:, 6, 0, :], ALU.add).then_inc(emptied["dve"], 1)
            def decayed_product(n):
                t, g = n // 4, (n % 4) // 2
                dve.wait_ge(emptied["act"], ORDINAL[f"acumb{n}"] + 1)
                dve.tensor_tensor(lmat[:, n % 4], lmat[:, n % 4], cb[:, 2 * t + g, :].unsqueeze(1).to_broadcast([P, 4, P]),
                                  ALU.mult).then_inc(mmat_done, 1)

            def state(g):
                dve.tensor_copy(prev[:, 512 * g:512 * g + 512], product(dve, f"state{g}")).then_inc(emptied["dve"], 1)

            def from_state(g):
                src = product(dve, f"yoff{g}").rearrange("p (h n) -> p h n", h=HG)
                dve.wait_ge(decay_done, 2)
                dve.tensor_tensor(yoff[:, 512 * g:512 * g + 512].rearrange("p (h n) -> p h n", h=HG), src,
                                  sp[:, 3, 1, HG * g:HG * g + HG].unsqueeze(2).to_broadcast([P, HG, HD]),
                                  ALU.mult).then_inc(emptied["dve"], 1)

            def ssd_out(n):
                t, g = n // 2, n % 2
                src = product(dve, f"ydiag{n}")
                cols = slice(512 * g, 512 * g + 512)
                dve.wait_ge(xskip_done, 2)
                dve.tensor_tensor(y[:, t, cols], src, xs[:, t, cols], ALU.add).then_inc(emptied["dve"], 1)
                dve.wait_ge(emptied["dve"], ORDINAL[f"ydiag{n}"] + 1)
                if t == 1:
                    settle(dve.tensor_tensor(y[:, t, cols], y[:, t, cols], yoff[:, cols], ALU.add))

            for n in range(4):
                decayed_product(n)
            for g in range(GROUPS):
                state(g)
            for g in range(GROUPS):
                from_state(g)
            ssd_out(0)
            decayed_product(4)
            decayed_product(5)
            ssd_out(1)
            decayed_product(6)
            decayed_product(7)
            ssd_out(2)
            ssd_out(3)
            for t in range(TT):
                dve.tensor_tensor(y[:, t, :], y[:, t, :], zs[:, t, :], ALU.mult).then_inc(yz_done, 1)
            dve.wait_ge(y_sq, 4)
            mean_eps(slice(12, 16), slice(16, 20), 512, y_ms)
            dve.wait_ge(y_rt, 1)
            settle(dve.reciprocal(stat[:, 16:20], stat[:, 16:20]))
            for t in range(TT):
                for g in range(GROUPS):
                    yg = y[:, t, 512 * g:512 * g + 512]
                    dve.tensor_scalar(yg, yg, stat[:, 16 + 2 * t + g:17 + 2 * t + g], None, ALU.mult).then_inc(yn_done, 1)
            for n in range(4):
                t, h = n % 2, n // 2
                src = product(dve, f"yT{n}").rearrange("p (k t) -> p k t", k=4)
                dve.tensor_tensor(yT[:, 4 * h:4 * h + 4, P * t:P * t + P], src,
                                  gssd[:, 4 * h:4 * h + 4].unsqueeze(2).to_broadcast([P, 4, P]),
                                  ALU.mult).then_inc(emptied["dve"], 1)
            for n in range(4):
                t, s = n % 2, n // 2
                cols = slice(512 * s, 512 * s + 512)
                dve.tensor_tensor(y[:, t, cols], product(dve, f"ssdout{n}"), gate[:, t, cols], ALU.mult).then_inc(emptied["dve"], 1)

            def score_max(n):
                j, _, hs = SCORES[n]
                src = product(dve, f"S{n}")[:, 0:hs * P * (j + 1)].rearrange("p (h k) -> p h k", h=hs)
                settle(dve.tensor_reduce(nmax[:, n, 0:hs], src, AX.X, ALU.max))
                dve.tensor_scalar(nmax[:, n, 0:hs], nmax[:, n, 0:hs], -SCALE, None, ALU.mult).then_inc(max_done, 1)

            def normalise(n):
                j, _, hs = SCORES[n]
                dve.wait_ge(emptied["act"], ORDINAL[f"S{n}"] + 1)
                settle(dve.reciprocal(psums[:, n, 0:hs], psums[:, n, 0:hs]))
                pv = prob[:, n % 3, :].rearrange("p (h k) -> p h k", h=hs)
                dve.tensor_tensor(pv, pv, psums[:, n, 0:hs].unsqueeze(2).to_broadcast([P, hs, P * (j + 1)]), ALU.mult).then_inc(prob_done, 1)

            def heads_out(n):
                j, h0, hs = SCORES[n]
                src = product(dve, f"O{n}")[:, 0:hs * P].rearrange("p (h q) -> p h q", h=hs)
                dve.tensor_copy(oT[:, h0:h0 + 2 * hs - 1:2, P * j:P * j + P], src).then_inc(emptied["dve"], 1)

            for name, _ in PRODUCTS[INDEX["S0"]:INDEX["O5"] + 1]:
                n = int(name[-1])
                if name[0] == "S":
                    score_max(n)
                    normalise(n)
                elif name[0] == "O":
                    heads_out(n)
            for n in range(4):
                t, s = n % 2, n // 2
                cols = slice(512 * s, 512 * s + 512)
                src = product(dve, f"mlaout{n}")
                gcols = gate[:, t, D + 512 * s:D + 512 * s + 512]
                dve.tensor_tensor(gcols, src, gcols, ALU.mult).then_inc(emptied["dve"], 1)
                dve.wait_ge(emptied["dve"], ORDINAL[f"mlaout{n}"] + 1)
                dve.tensor_tensor(y[:, t, cols], y[:, t, cols], gcols, ALU.add).then_inc(merged, 1)
            for n in range(4):
                t, s = n % 2, n // 2
                cols = slice(512 * s, 512 * s + 512)
                src = product(dve, f"wo{n}")
                dve.tensor_tensor(resid[:, t, cols], src, resid[:, t, cols], ALU.add).then_inc(emptied["dve"], 1)
            dve.wait_ge(emptied["dve"], ORDINAL["wo3"] + 1)
            dve.memset(stat[:, 61:62], 0.0).then_inc(w_free, RING)
            dve.memset(stat[:, 60:61], 0.0).then_inc(t_read, 1)
            dve.wait_ge(x2_sq, TT)
            mean_eps(slice(20, 22), slice(22, 24), D, x2_ms)
            dve.wait_ge(x2_rt, 1)
            settle(dve.reciprocal(stat[:, 22:24], stat[:, 22:24]))
            dve.wait_ge(late_in, 5 * 16)
            for t in range(TT):
                dve.scalar_tensor_tensor(out=h2[:, t, :], in0=resid[:, t, :], scalar=stat[:, 22 + t:23 + t],
                                         in1=gain_ffn[:, :], op0=ALU.mult, op1=ALU.mult).then_inc(h2_done, 1)
            dve.wait_ge(h2_done, 2)
            for t in range(TT):
                settle(dve.tensor_copy(h2hi[:, t, :], h2[:, t, :]))
                dve.tensor_tensor(h2lo[:, t, :], h2[:, t, :], h2hi[:, t, :].bitcast(F32), ALU.subtract).then_inc(h2_split, 1)
            def low_part(G, i, j):
                n = nth(i, j)
                dve.wait_ge(hi_done, G * (GE * EJ) + n + 1)
                dve.tensor_tensor(low_slot(n), ring_slot(n), high_slot(n).bitcast(F32), ALU.subtract).then_inc(lo_done, 1)

            dve.memset(giveT[:, :, :], 0.0).then_inc(zeroed, 1)
            low_part(0, -1, 6)
            low_part(0, -1, 7)
            src = product(dve, "logits")[:, 0:TT * EXPERTS].rearrange("p (t e) -> p t e", t=TT)
            dve.tensor_tensor(lg[:, :, :], src, brouter[:, :].unsqueeze(1).to_broadcast([P, TT, EXPERTS]), ALU.add).then_inc(emptied["dve"], 1)
            dve.wait_ge(emptied["dve"], ORDINAL["logits"] + 1)
            for t in range(TT):
                settle(dve.max(out=top[:, t, :], in_=lg[:, t, :]))
                settle(dve.max_index(out=topi[:, t, :], in_max=top[:, t, :], in_values=lg[:, t, :]))
                settle(dve.tensor_copy(topf[:, t, :], topi[:, t, :]))
                dve.tensor_scalar(tg[:, t, 4:5], top[:, t, 0:1], -1.0, None, ALU.mult).then_inc(top_done, 1)
            dve.wait_ge(top_exp, 2)
            for t in range(TT):
                settle(dve.reciprocal(tg[:, t, 6:7], tg[:, t, 5:6]))
                settle(dve.tensor_scalar(tg[:, t, 0:4], tg[:, t, 0:4], tg[:, t, 6:7], None, ALU.mult))
                settle(dve.tensor_tensor(onehot[:, :, :], iota_e[:, :].unsqueeze(1).to_broadcast([P, TOPK, EXPERTS]),
                                         topf[:, t, 0:TOPK].unsqueeze(2).to_broadcast([P, TOPK, EXPERTS]), ALU.is_equal))
                settle(dve.tensor_reduce(picked[:, t, :], onehot[:, :, :].rearrange("p k e -> p e k"), AX.X, ALU.add))
                dve.tensor_copy(pickedb[:, t, :], picked[:, t, :]).then_inc(picked_done, 1)
                settle(dve.tensor_tensor(onehot[:, :, :], onehot[:, :, :], tg[:, t, 0:TOPK].unsqueeze(2).to_broadcast([P, TOPK, EXPERTS]), ALU.mult))
                dve.tensor_reduce(gates[:, t, 0:EXPERTS], onehot[:, :, :].rearrange("p k e -> p e k"), AX.X, ALU.add).then_inc(gates_done, 1)
            dve.wait_ge(gates_done, 2)
            dve.tensor_copy(gates[:, :, EXPERTS:EXPERTS + GE], gates[:, :, 0:GE])
            src = product(dve, "rank")
            rank = src[:, 0:TT * EXPERTS].rearrange("p (t e) -> p t e", t=TT)
            settle(dve.scalar_tensor_tensor(out=picked[:, :, :], in0=rank, scalar=1.0, in1=picked[:, :, :], op0=ALU.add, op1=ALU.mult))
            dve.tensor_reduce(load[:, 0:1], src[:, TT * EXPERTS:(TT + 1) * EXPERTS], AX.X, ALU.max).then_inc(emptied["dve"], 1)
            for b in range(PASSES):
                settle(dve.tensor_scalar(pos[:, :, EXPERTS * b:EXPERTS * b + EXPERTS], picked[:, :, :], -1.0 - CAP * b, None, ALU.add))
                if b == 0:
                    for t in range(TT):
                        for i in range(GE):
                            ins = dve.tensor_scalar(pick[:, t, CAP * i:CAP * i + CAP], slot_no[:, 0:CAP], pos[:, t, i:i + 1],
                                                    None, ALU.is_equal)
                    ins.then_inc(pick_ready, 1)
            dve.memset(pos[:, :, PASSES * EXPERTS:], -1.0)
            dve.wait_ge(emptied["dve"], ORDINAL["rank"] + 1)
            settle(dve.tensor_scalar(load[:, 1:2], load[:, 0:1], float(CAP), float(EXPERTS), ALU.is_gt, ALU.mult))
            settle(dve.tensor_scalar(load[:, 2:3], load[:, 0:1], 2.0 * CAP, float(EXPERTS), ALU.is_gt, ALU.mult))
            settle(dve.tensor_scalar(load[:, 3:4], load[:, 0:1], 3.0 * CAP, float(EXPERTS), ALU.is_gt, ALU.mult))
            settle(dve.tensor_tensor(load[:, 1:2], load[:, 1:2], load[:, 2:3], ALU.add))
            settle(dve.scalar_tensor_tensor(out=load[:, 1:2], in0=load[:, 1:2], scalar=float(EXPERTS), in1=load[:, 3:4], op0=ALU.add, op1=ALU.add))
            dve.tensor_copy(loadi[:, :], load[:, 0:2]).then_inc(routed, 1)
            dve.tensor_copy(gatesT[:, :], product(dve, "gatesT")[0:EXPERTS, 0:TOKENS]).then_inc(emptied["dve"], 1)
            low_part(0, -1, 9)
            for n in range(4):
                t, s = n % 2, n // 2
                cols = slice(512 * s, 512 * s + 512)
                src = product(dve, f"bias{n}")
                dve.tensor_tensor(resid[:, t, cols], src, resid[:, t, cols], ALU.add).then_inc(emptied["dve"], 1)

            dve.wait_ge(emptied["dve"], ORDINAL["bias3"] + 1)
            dve.memset(psy[:, :, :], 0.0).then_inc(zeroed, 1)
            dve.wait_ge(routed, 1)
            load_max = dve.value_load(loadi[0:1, 0:1], min_val=0, max_val=TOKENS)
            runs = dve.value_load(loadi[0:1, 1:2], min_val=0, max_val=PASSES * EXPERTS)

            def glu_begin(G, i, hf):
                n = G * (2 * GE) + 2 * i + hf + 1
                dve.wait_ge(t_filled, n)
                bias = bias_of(i, hf)
                dve.tensor_tensor(gu[:, :, :], pst[:, :].rearrange("p (c s) -> p c s", c=8),
                                  bias, ALU.add).then_inc(t_read, 1)
                dve.wait_ge(t_read, n + 1)
                dve.tensor_scalar(gu[:, 0:4, :], gu[:, 0:4, :], LIMIT, None, ALU.min).then_inc(glu_done, 1)
                dve.tensor_scalar(lin[:, :, :], gu[:, 4:8, :], LIMIT, -LIMIT, ALU.min, ALU.max).then_inc(lin_done, 1)

            def glu_end(G, i, hf):
                n = G * (2 * GE) + 2 * i + hf + 1
                dve.wait_ge(lin_done, n)
                dve.scalar_tensor_tensor(out=lin[:, :, :], in0=lin[:, :, :], scalar=1.0, in1=gu[:, 0:4, :],
                                         op0=ALU.add, op1=ALU.mult).then_inc(prod_done, 1)
                dve.wait_ge(prod_done, n)
                dve.wait_ge(sig_done, n)
                dve.tensor_tensor(af[:, :, :], lin[:, :, :], sg[:, :, :], ALU.mult).then_inc(af_done, 1)
                dve.wait_ge(af_done, n)
                ks = slice(4 * hf, 4 * hf + 4)
                dve.tensor_copy(actT[:, ks, 0:CAP], af[:, :, :]).then_inc(ahi_done, 1)
                dve.wait_ge(ahi_done, n)
                dve.tensor_tensor(actT[:, ks, CAP:P], af[:, :, :], actT[:, ks, 0:CAP].bitcast(F32),
                                  ALU.subtract).then_inc(act_ready, 1)

            def add_scattered(before, p):
                t, s = p // 2, p % 2
                cols = slice(512 * s, 512 * s + 512)
                dve.wait_ge(sc_filled, before + 1)
                dve.tensor_tensor(resid[:, t, cols], ps[s][:, :], resid[:, t, cols], ALU.add).then_inc(y_added, 1)

            with dve.Fori(0, PASSES) as b:
                with dve.If(load_max > b * CAP):
                    with dve.Fori(0, NG) as g:
                        G = b * NG + g

                        def bias_of(i, hf):
                            v = bgu[:, bass.ds(g * GE + i, 1), 8 * hf:8 * hf + 8]
                            return v.rearrange("p e c -> p (e c)").unsqueeze(2).to_broadcast([P, 8, CAP])

                        for i in range(GE):
                            E = G * GE + i
                            events = {4: lambda: glu_begin(G, i, 0), 5: lambda: glu_end(G, i, 0),
                                      9: lambda: glu_begin(G, i, 1), 10: lambda: glu_end(G, i, 1)}
                            for j in range(EJ):
                                if j in DVE_PLACES:
                                    low_part(G, i, j)
                                if j in events:
                                    events[j]()
                                if j == (5 if i % 2 else 6):
                                    add_scattered(E * 2, 2 * (i % 2))
                                    add_scattered(E * 2 + 1, 2 * (i % 2) + 1)
            for p in range(4):
                add_scattered(runs * 2 + p, p)

        @block.tensor
        def _(pe):
            def begin(name):
                n = INDEX[name]
                if n >= 8:
                    before, who = PRODUCTS[n - 8]
                    pe.wait_ge(emptied[who], ORDINAL[before] + 1)
                return bank(name)

            def landed(n):
                pe.wait_ge(raw_in[n % RAW], raw_in_count(n))

            pe.wait_ge(consts, 1)
            for n in range(4):
                t, h = n % 2, n // 2
                pe.wait_ge(xn_done, t + 1)
                o = begin(f"hT{n}")
                for k in range(4):
                    kk = 4 * h + k
                    ins = pe.transpose(o[:, P * k:P * k + P], xn[:, t, P * kk:P * kk + P], ident[:, :])
                ins.then_inc(filled, 1)
            pe.wait_ge(emptied["dve"], ORDINAL["hT3"] + 1)

            def tokens_product(name, src, t, slots, c0, width, release_slots=False):
                o = begin(name)
                total = sum(FRONT_SLOTS[s][2] for s in slots)
                k = 0
                for s in slots:
                    landed(s)
                    for kk in range(FRONT_SLOTS[s][2]):
                        ins = pe.matmul(o[:, 0:width], src[:, k, P * t:P * t + P],
                                        front_slot(s)[:, kk, c0:c0 + width], start=(k == 0), stop=(k == total - 1))
                        k += 1
                ins.then_inc(filled, 1)
                return ins

            slot = 0
            for part, width in ((0, CA), (1, CB_)):
                for t in range(TT):
                    ins = tokens_product(f"lat{2 * part + t}", hT, t, (slot, slot + 1), 0, width)
                slot += 2
            for s in range(3):
                for half in range(2):
                    n = 2 * s + half
                    o = begin(f"xbc{n}")
                    for c in range(2):
                        for k in range(KD):
                            sl = slot + k // 4
                            if c == 0:
                                landed(sl)
                            cc = P * (2 * half + c)
                            ins = pe.matmul(o[:, TOKENS * c:TOKENS * c + TOKENS], front_slot(sl)[:, k % 4, cc:cc + P],
                                            hT[:, k, :], start=(k == 0), stop=(k == KD - 1))
                    ins.then_inc(filled, 1)
                slot += 2
            for s in range(2):
                for t in range(TT):
                    ins = tokens_product(f"z{2 * s + t}", hT, t, (slot, slot + 1), 0, 512)
                slot += 2
            pe.wait_ge(lat_done, 2 * TT)
            for n in range(4):
                t, part = n % 2, n // 2
                c0, kk = (HEADS, 3) if part == 0 else (CA, 2)
                o = begin(f"latT{n}")
                for k in range(kk):
                    ins = pe.transpose(o[:, P * k:P * k + P], lat[:, t, c0 + P * k:c0 + P * k + P], ident[:, :])
                ins.then_inc(filled, 1)
            pe.wait_ge(emptied["dve"], ORDINAL["latT3"] + 1)
            latT = latent_T
            for s in range(3):
                for t in range(TT):
                    ins = tokens_product(f"qup{2 * s + t}", latT[:, 0:3], t, (slot,), 0, 512)
                slot += 1
            for s in range(4):
                for t in range(TT):
                    ins = tokens_product(f"kvup{2 * s + t}", latT[:, 3:5], t, (slot,), 512 * (s % 2), 512)
                if s % 2:
                    slot += 1
            for s in range(4):
                for t in range(TT):
                    ins = tokens_product(f"gate{2 * s + t}", hT, t, (slot, slot + 1), 0, 512)
                slot += 2
            pe.wait_ge(silu_done, 3)
            for n in range(4):
                t, h = n % 2, n // 2
                o = begin(f"xsT{n}")
                for k in range(4):
                    ins = pe.transpose(o[:, P * k:P * k + P], xc[:, 4 * h + k, P * t:P * t + P], ident[:, :])
                ins.then_inc(filled, 1)
            o = begin("btok")
            for g in range(GROUPS):
                ins = pe.transpose(o[:, P * g:P * g + P], xc[:, KD + g, 0:P], ident[:, :])
            ins.then_inc(filled, 1)
            o = begin("cb")
            for t in range(TT):
                for g in range(GROUPS):
                    a = P * (2 * t + g)
                    ins = pe.matmul(o[:, a:a + P], xc[:, KD + g, P * t:P * t + P], xc[:, KD + GROUPS + g, P * t:P * t + P],
                                    start=True, stop=True)
            ins.then_inc(filled, 1)
            pe.wait_ge(dt_done, 1)
            o = begin("acum")
            for t in range(TT):
                pe.matmul(o[:, HEADS * t:HEADS * t + HEADS], upper[:, :], sp[:, 5, t, :], start=True, stop=True)
            pe.matmul(o[:, 2 * HEADS:3 * HEADS], ones[:, :], sp[:, 5, 0, :], start=True, stop=True).then_inc(filled, 1)

            def cumulated(n):
                t = n // 4
                o = begin(f"acumb{n}")
                for hh in range(4):
                    h = 4 * (n % 4) + hh
                    v = o[:, P * hh:P * hh + P]
                    pe.matmul(v, sp[:, 5, t, h:h + 1].to_broadcast([P, P]), upper[:, :], start=True, stop=False)
                    ins = pe.matmul(v, identb[:, :], causal[:, :], start=False, stop=True)
                ins.then_inc(filled, 1)

            def state(g):
                o = begin(f"state{g}")
                pe.matmul(o, btok[:, P * g:P * g + P], xdec[:, 512 * g:512 * g + 512], start=True, stop=True).then_inc(filled, 1)

            def from_state(g):
                o = begin(f"yoff{g}")
                pe.matmul(o, xc[:, KD + GROUPS + g, P:2 * P], prev[:, 512 * g:512 * g + 512], start=True, stop=True).then_inc(filled, 1)

            def ssd_out(n):
                t, g = n // 2, n % 2
                o = begin(f"ydiag{n}")
                for half in range(2):
                    m = 2 * n + half
                    pe.wait_ge(mmat_done, m + 1)
                    for hh in range(4):
                        c = HD * (4 * half + hh)
                        ins = pe.matmul(o[:, c:c + HD], lmat[:, m % 4, hh, :], xdt[:, t, 512 * g + c:512 * g + c + HD],
                                        start=True, stop=True)
                ins.then_inc(filled, 1)

            for n in range(4):
                cumulated(n)
            pe.wait_ge(xdt_done, 1)
            for g in range(GROUPS):
                state(g)
            pe.wait_ge(emptied["dve"], ORDINAL["state1"] + 1)
            for g in range(GROUPS):
                from_state(g)
            ssd_out(0)
            cumulated(4)
            cumulated(5)
            ssd_out(1)
            cumulated(6)
            cumulated(7)
            ssd_out(2)
            ssd_out(3)
            pe.wait_ge(q_done, TT)
            for n in range(6):
                t, part = n % 2, n // 2
                o = begin(f"qT{n}")
                for k in range(4):
                    src = qb[:, t, 4 * part + k, 0:NOPE] if part < 2 else qr[:, t, P * k:P * k + P]
                    ins = pe.transpose(o[:, P * k:P * k + P], src, ident[:, :])
                ins.then_inc(filled, 1)
            pe.wait_ge(yn_done, 4)
            for n in range(4):
                t, h = n % 2, n // 2
                o = begin(f"yT{n}")
                for k in range(4):
                    kk = 4 * h + k
                    ins = pe.transpose(o[:, P * k:P * k + P], y[:, t, P * kk:P * kk + P], ident[:, :])
                ins.then_inc(filled, 1)
            pe.wait_ge(emptied["dve"], ORDINAL["yT3"] + 1)
            for s in range(2):
                for t in range(TT):
                    ins = tokens_product(f"ssdout{2 * s + t}", yT, t, (slot, slot + 1), 0, 512)
                slot += 2
            pe.wait_ge(k_done, TT)
            for n in range(6):
                t, part = n % 2, n // 2
                o = begin(f"kT{n}")
                for k in range(4):
                    src = kv[:, t, 4 * part + k, 0:NOPE] if part < 2 else kr[:, t, 2 * k:2 * k + 2, :].rearrange("p h n -> p (h n)")
                    ins = pe.transpose(o[:, P * k:P * k + P], src, ident[:, :])
                ins.then_inc(filled, 1)
            pe.wait_ge(emptied["act"], ORDINAL["kT5"] + 1)

            def scores(n):
                j, h0, hs = SCORES[n]
                keys = P * (j + 1)
                o = begin(f"S{n}")
                qs = slice(P * j, P * j + P)
                for hh in range(hs):
                    h = h0 + 2 * hh
                    a = keys * hh
                    half = slice(64 * (h % 2), 64 * (h % 2) + 64)
                    pe.matmul(o[:, a:a + keys], qT[:, h, qs], kT[:, h, 0:keys], start=True, stop=False)
                    pe.matmul(o[:, a:a + keys], qrT[half, h // 2, qs], krT[half, h // 2, 0:keys], start=False, stop=False)
                    ins = pe.matmul(o[:, a:a + keys], identb[:, :], amask[:, 2 * P - keys:2 * P], start=False, stop=True)
                ins.then_inc(filled, 1)

            def turn_probs(n):
                j, _, hs = SCORES[n]
                pe.wait_ge(prob_done, n + 1)
                o = begin(f"PT{n}")
                for k in range(4):
                    ins = pe.transpose(o[:, P * k:P * k + P], prob[:, n % 3, P * k:P * k + P], ident[:, :])
                ins.then_inc(filled, 1)

            def values(n):
                j, h0, hs = SCORES[n]
                pe.wait_ge(emptied["act"], ORDINAL[f"PT{n}"] + 1)
                o = begin(f"O{n}")
                for hh in range(hs):
                    for kt in range(j + 1):
                        a = P * ((j + 1) * hh + kt)
                        ins = pe.matmul(o[:, P * hh:P * hh + P], kv[:, kt, h0 + 2 * hh, NOPE:NOPE + VD],
                                        probT[:, n % 3, a:a + P], start=(kt == 0), stop=(kt == j))
                ins.then_inc(filled, 1)

            for name, _ in PRODUCTS[INDEX["S0"]:INDEX["O5"] + 1]:
                {"S": scores, "P": turn_probs, "O": values}[name[0]](int(name[-1]))
            pe.wait_ge(emptied["dve"], ORDINAL["O5"] + 1)
            for s in range(2):
                for t in range(TT):
                    ins = tokens_product(f"mlaout{2 * s + t}", oT, t, (slot, slot + 1), 0, 512)
                slot += 2
            for n in range(4):
                t, h = n % 2, n // 2
                pe.wait_ge(merged, n + 1)
                o = begin(f"mT{n}")
                for k in range(4):
                    kk = 4 * h + k
                    ins = pe.transpose(o[:, P * k:P * k + P], y[:, t, P * kk:P * kk + P], ident[:, :])
                ins.then_inc(filled, 1)
            pe.wait_ge(emptied["act"], ORDINAL["mT3"] + 1)
            for s in range(2):
                for t in range(TT):
                    ins = tokens_product(f"wo{2 * s + t}", mT, t, (slot, slot + 1), 0, 512)
                slot += 2
            assert slot == NF
            for n in range(4):
                t, h = n % 2, n // 2
                pe.wait_ge(h2_done, t + 1)
                o = begin(f"h2T{n}")
                for k in range(4):
                    kk = 4 * h + k
                    ins = pe.transpose(o[:, P * k:P * k + P], h2[:, t, P * kk:P * kk + P], ident[:, :])
                ins.then_inc(filled, 1)
            pe.wait_ge(emptied["act"], ORDINAL["h2T3"] + 1)
            pe.wait_ge(late_in, 5 * 16)
            o = begin("logits")
            for t in range(TT):
                for k in range(KD):
                    ins = pe.matmul(o[:, EXPERTS * t:EXPERTS * t + EXPERTS], h2T[:, k, P * t:P * t + P], wrouter[:, k, :],
                                    start=(k == 0), stop=(k == KD - 1))
            ins.then_inc(filled, 1)
            pe.wait_ge(picked_done, 2)
            o = begin("rank")
            pe.matmul(o[:, 0:EXPERTS], strictb[:, :], pickedb[:, 0, :], start=True, stop=True)
            pe.matmul(o[:, EXPERTS:2 * EXPERTS], onesb[:, :], pickedb[:, 0, :], start=True, stop=False)
            pe.matmul(o[:, EXPERTS:2 * EXPERTS], strictb[:, :], pickedb[:, 1, :], start=False, stop=True)
            pe.matmul(o[:, 2 * EXPERTS:3 * EXPERTS], onesb[:, :], pickedb[:, 0, :], start=True, stop=False)
            pe.matmul(o[:, 2 * EXPERTS:3 * EXPERTS], onesb[:, :], pickedb[:, 1, :], start=False, stop=True).then_inc(filled, 1)
            pe.wait_ge(gates_done, 2)
            o = begin("gatesT")
            for t in range(TT):
                ins = pe.transpose(o[0:EXPERTS, P * t:P * t + P], gates[:, t, 0:EXPERTS], ident[:, :])
            ins.then_inc(filled, 1)
            def gather(k, to=psm):
                for part, src in enumerate((h2hi, h2lo)):
                    for t in range(TT):
                        ins = pe.matmul(to[:, 256 * part:256 * part + 256], src[:, t, P * k:P * k + P], pick[:, t, :],
                                        start=(t == 0), stop=(t == TT - 1))
                ins.then_inc(x_filled, 1)

            def split_landed(G, i, j):
                if j in POOL_PLACES:
                    pe.wait_ge(lo_done_pool, low_order(POOL_PLACES, POOL_FIRST, G, i, j))
                else:
                    pe.wait_ge(lo_done, low_order(DVE_PLACES, DVE_FIRST, G, i, j))

            def gate_up_chunk(i, n, k, hf):
                for part, w in enumerate((high_slot(n), low_slot(n))):
                    for s in range(2):
                        o = ps[s][:, :] if hf == 0 else ps2[:, s, :]
                        a = D * (k % 2) + 512 * s
                        ins = pe.matmul(o, xT[:, k, i, :], w[:, a:a + 512],
                                        start=(k == 0 and part == 0), stop=(k == KD - 1 and part == 1))
                return ins

            def first_half_slot(G, i, j):
                split_landed(G, i, j)
                for k in (2 * (j - 6), 2 * (j - 6) + 1):
                    if i in (-1, GE - 1):
                        pe.wait_ge(x_out, (G + (i > 0)) * KD + k + 1)
                    ins = gate_up_chunk((i + 1) % GE, nth(i, j), k, 0)
                    if i < 0 and k < KD - 2:
                        gather(k + 2, (psm, pst)[k % 2])
                ins.then_inc(w_free, 1)

            def down_slot(G, i, j):
                split_landed(G, i, j)
                n = nth(i, j)
                for k2 in range(2):
                    k = 2 * (j - 4 if j < 6 else j - 8) + k2
                    for part, w in enumerate((high_slot(n), low_slot(n))):
                        for s in range(2):
                            a = D * k2 + 512 * s
                            ins = pe.matmul(psy[:, s, :], actT[:, k, :], w[:, a:a + 512],
                                            start=(k == 0 and part == 0), stop=(k == KD - 1 and part == 1))
                ins.then_inc(w_free, 1)

            def turn_sums(G, i, hf):
                pe.wait_ge(gu_out, G * (4 * GE) + 4 * i + 2 * hf + 2)
                pe.wait_ge(t_read, G * (2 * GE) + 2 * i + hf + 1)
                for c in range(8):
                    ins = pe.matmul(pst[:, CAP * c:CAP * c + CAP], gusb[:, hf, P * c:P * c + P], stacked[:, :],
                                    start=True, stop=True)
                ins.then_inc(t_filled, 1)

            def turn_gates(E, i):
                pe.wait_ge(give_ready, E + 1)
                for t in range(TT):
                    ins = pe.transpose(psm[:, P * t:P * t + P], give[:, i, t, :], ident[:, :])
                ins.then_inc(g_filled, 1)

            def scatter(p, first):
                t, s = p // 2, p % 2
                for m in range(2):
                    ins = pe.matmul(ps[s][:, :], giveT[:, (first + m) % GE, P * t:P * t + P],
                                    ysb[:, m, 512 * s:512 * s + 512], start=(m == 0), stop=(m == 1))
                ins.then_inc(sc_filled, 1)

            pe.wait_ge(h2_split, 2)
            pe.wait_ge(pick_ready, 1)
            gather(0, psm)
            gather(1, pst)
            for j in range(6, 10):
                first_half_slot(0, -1, j)
            pe.wait_ge(emptied["dve"], ORDINAL["gatesT"] + 1)
            for n in range(4):
                t, s = n % 2, n // 2
                o = begin(f"bias{n}")
                pe.matmul(o, gatesT[:, P * t:P * t + P], bdown[:, 512 * s:512 * s + 512], start=True, stop=True).then_inc(filled, 1)

            pe.wait_ge(emptied["dve"], ORDINAL["bias3"] + 1)
            load_max = pe.value_load(loadi[0:1, 0:1], min_val=0, max_val=TOKENS)
            runs = pe.value_load(loadi[0:1, 1:2], min_val=0, max_val=PASSES * EXPERTS)

            with pe.Fori(0, PASSES) as b:
                with pe.If(load_max > b * CAP):
                    with pe.Fori(0, NG) as g:
                        G = b * NG + g
                        for i in range(GE):
                            E = G * GE + i
                            if i:
                                pe.wait_ge(g_out, E)
                            turn_gates(E, i)
                            for j in range(4):
                                split_landed(G, i, j)
                                for k in (2 * j, 2 * j + 1):
                                    ins = gate_up_chunk(i, nth(i, j), k, 1)
                                    if k % 2:
                                        ins.then_inc(w_free, 1)
                                    if i == GE - 1:
                                        if k == 0:
                                            pe.wait_ge(pick_ready, G + 2)
                                            pe.wait_ge(g_out, E + 1)
                                        else:
                                            pe.wait_ge(x_out, G * KD + KD + k)
                                        gather(k)
                                if j == 1:
                                    turn_sums(G, i, 0)
                                    if i % 2:
                                        scatter(2, i - 3)
                                        scatter(3, i - 3)
                            if i % 2 == 0:
                                pe.wait_ge(y_out, E + 1)
                                pe.wait_ge(g_out, E)
                                scatter(0, i - 2)
                                scatter(1, i - 2)
                            pe.wait_ge(y_out, E + 1)
                            pe.wait_ge(act_ready, G * (2 * GE) + 2 * i + 1)
                            down_slot(G, i, 4)
                            down_slot(G, i, 5)
                            pe.wait_ge(y_added, 2 * E + 2)
                            first_half_slot(G, i, 6)
                            turn_sums(G, i, 1)
                            for j in (7, 8, 9):
                                first_half_slot(G, i, j)
                            pe.wait_ge(act_ready, G * (2 * GE) + 2 * i + 2)
                            down_slot(G, i, 10)
                            down_slot(G, i, 11)
            pe.wait_ge(y_out, runs + 1)
            pe.wait_ge(g_out, runs)
            scatter(0, GE - 2)
            scatter(1, GE - 2)
            pe.wait_ge(y_added, runs * 2 + 1)
            scatter(2, GE - 2)
            pe.wait_ge(y_added, runs * 2 + 2)
            scatter(3, GE - 2)


def kernel(x, g_mix, w_in, conv_w, conv_b, dt_bias, a_log, d_skip, g_ssd_out, w_ssd_out, g_q_lat, w_q_up,
           g_kv_lat, w_kv_up, g_qk_q, g_qk_k, w_mla_out, w_o, g_ffn, w_router, b_router, w_gate_up,
           b_gate_up, w_down, b_down):
    import concourse.bacc as bacc
    from concourse.bass_utils import run_bass_kernel_spmd

    def columns(v, n):
        return np.asarray(v).reshape(n, P).T

    def rows(v):
        v = np.asarray(v).reshape(1, -1)
        return np.repeat(v, P, axis=0)

    pos = np.arange(TOKENS, dtype=np.float32)
    inv = (np.float32(10000.0) ** (-np.arange(0, ROPE, 2, dtype=np.float32) / np.float32(ROPE))).astype(np.float32)
    ang = (pos[:, None] * inv[None, :]).astype(np.float32)

    def table(a):
        return a.astype(np.float32).reshape(TT, P, ROPE // 2).transpose(1, 0, 2)

    host = {
        "x": np.asarray(x)[0],
        "w_in": np.asarray(w_in)[0], "w_q_up": np.asarray(w_q_up)[0], "w_kv_up": np.asarray(w_kv_up)[0],
        "w_ssd_out": np.asarray(w_ssd_out)[0], "w_mla_out": np.asarray(w_mla_out)[0], "w_o": np.asarray(w_o)[0],
        "w_router": np.asarray(w_router)[0].reshape(KD, P, EXPERTS).transpose(1, 0, 2),
        "w_gate_up": np.asarray(w_gate_up)[0].reshape(EXPERTS, 4, 2, P, 2, 2, 512).transpose(0, 5, 1, 3, 2, 4, 6)
        .reshape(EXPERTS, 8, P, SLOT),
        "w_down": np.asarray(w_down)[0].reshape(EXPERTS, 4, 2, P, D).transpose(0, 1, 3, 2, 4).reshape(EXPERTS, 4, P, SLOT),
        "g_mix": columns(g_mix, KD), "conv_w": np.asarray(conv_w)[0].reshape(CONV, XC, P).transpose(2, 1, 0),
        "conv_b": columns(conv_b, XC), "dt_bias": rows(dt_bias), "a_log": rows(a_log), "d_skip": rows(d_skip),
        "g_ssd_out": columns(g_ssd_out, KD), "g_q_lat": columns(g_q_lat, 3), "g_kv_lat": columns(g_kv_lat, 2),
        "g_qk_q": rows(g_qk_q), "g_qk_k": rows(g_qk_k), "g_ffn": rows(g_ffn), "b_router": rows(b_router),
        "b_gate_up": np.asarray(b_gate_up)[0].reshape(EXPERTS, 2, 2, 4, P).transpose(4, 0, 2, 1, 3).reshape(P, EXPERTS, 16),
        "b_down": np.asarray(b_down)[0],
        "cos": table(np.cos(ang)), "sin": table(np.sin(ang)),
    }
    nc = bacc.Bacc("TRN2", target_bir_lowering=False, num_devices=1)
    arrays, args = {}, {}
    for name, a in host.items():
        a = np.ascontiguousarray(a)
        arrays[f"in_{name}"] = a
        args[name] = nc.dram_tensor(f"in_{name}", a.shape, mybir.dt.from_np(a.dtype), kind="ExternalInput").ap()
    out = nc.dram_tensor("out_x", (TOKENS, D), F32, kind="ExternalOutput").ap()
    build(nc, out=out, **args)
    r = run_bass_kernel_spmd(nc, [arrays], core_ids=[0])
    return r.results[0]["out_x"].reshape(1, TOKENS, D)
```

```python
from contextlib import ExitStack

import numpy as np
import concourse.bass as bass
from concourse import mybir

F32 = mybir.dt.float32
F32R = mybir.dt.float32r
BF16 = mybir.dt.bfloat16
I32 = mybir.dt.int32
U32 = mybir.dt.uint32
ALU = mybir.AluOpType
ACT = mybir.ActivationFunctionType
AX = mybir.AxisListType

P = 128
D = 1024
TOKENS = 256
TT = TOKENS // P
KD = D // P
EPS = 1e-6

HEADS = 16
HD = 64
GROUPS = 2
HG = HEADS // GROUPS
STATE = 128
CONV = 4
XBC = D + 2 * GROUPS * STATE
XC = XBC // P
OFF_XBC = D
OFF_DT = OFF_XBC + XBC

AH = 8
QR, KVR = 384, 256
NOPE, ROPE, VD = 128, 64, 128
QK = NOPE + ROPE
OFF_Q = OFF_DT + HEADS
OFF_KV = OFF_Q + QR
OFF_KR = OFF_KV + KVR
OFF_GATE = OFF_KR + ROPE
CA = HEADS + QR
CB_ = KVR + ROPE
LAT = CA + CB_
SCALE = QK ** -0.5
CHUNK = 64

EXPERTS = 32
TOPK = 4
CAP = 64
PASSES = TOKENS // CAP
ARENA = 32964
GE = 4
NG = EXPERTS // GE
ALPHA, LIMIT = 1.702, 7.0
NEG = -1e30

SLOT = 2048
RAW = 6
RING = 8
HIGHS = 4
EJ = 12
HALF = 4
POOL_PLACES = (2, 8)
DVE_PLACES = tuple(j for j in range(EJ) if j not in POOL_PLACES)
POOL_FIRST = sum(j in POOL_PLACES for j in range(6, 10))
DVE_FIRST = HALF - POOL_FIRST

FRONT_SLOTS = (
    [("w_in", k, 4, OFF_DT, CA, "lat1") for k in (0, 4)] + [("w_in", k, 4, OFF_KV, CB_, "lat3") for k in (0, 4)]
    + [("w_in", k, 4, OFF_XBC + 512 * s, 512, f"xbc{2 * s + 1}") for s in range(3) for k in (0, 4)]
    + [("w_in", k, 4, 512 * s, 512, f"z{2 * s + 1}") for s in range(2) for k in (0, 4)]
    + [("w_q_up", 0, 3, 512 * s, 512, f"qup{2 * s + 1}") for s in range(3)]
    + [("w_kv_up", 0, 2, 1024 * s, 1024, f"kvup{4 * s + 3}") for s in range(2)]
    + [("w_in", k, 4, OFF_GATE + 512 * s, 512, f"gate{2 * s + 1}") for s in range(4) for k in (0, 4)]
    + [("w_ssd_out", k, 4, 512 * s, 512, f"ssdout{2 * s + 1}") for s in range(2) for k in (0, 4)]
    + [("w_mla_out", k, 4, 512 * s, 512, f"mlaout{2 * s + 1}") for s in range(2) for k in (0, 4)]
    + [("w_o", k, 4, 512 * s, 512, f"wo{2 * s + 1}") for s in range(2) for k in (0, 4)])
NF = len(FRONT_SLOTS)

PRODUCTS = (
    [(f"hT{n}", "dve") for n in range(4)]
    + [(f"lat{n}", "act") for n in range(4)]
    + [(f"xbc{n}", "act") for n in range(6)]
    + [(f"z{n}", "act") for n in range(4)]
    + [(f"latT{n}", "dve") for n in range(4)]
    + [(f"qup{n}", "act") for n in range(6)]
    + [(f"kvup{n}", "act") for n in range(8)]
    + [(f"gate{n}", "act") for n in range(6)]
    + [(f"xsT{n}", "act") for n in range(4)]
    + [("btok", "dve"), ("cb", "dve"), ("acum", "dve")]
    + [(x, "act" if x[0] == "a" else "dve") for x in
       ("acumb0 acumb1 acumb2 acumb3 state0 state1 yoff0 yoff1 ydiag0 acumb4 acumb5 ydiag1 acumb6 acumb7 "
        "ydiag2 ydiag3".split())]
    + [(f"qT{n}", "act") for n in range(6)]
    + [(f"kT{n}", "act") for n in range(6)]
    + [("gate6", "act"), ("gate7", "act")]
    + [(f"yT{n}", "dve") for n in range(4)]
    + [(x, "act" if x[0] in "SP" else "dve") for x in
       ("S0 ssdout0 S1 S2 ssdout1 PT0 S3 PT1 ssdout2 O0 PT2 O1 S4 PT3 ssdout3 O2 S5 PT4 O3 PT5 O4 O5".split())]
    + [(f"mlaout{n}", "dve") for n in range(4)]
    + [(f"mT{n}", "act") for n in range(4)]
    + [(f"wo{n}", "dve") for n in range(4)]
    + [(f"h2T{n}", "act") for n in range(4)]
    + [("logitsT", "dve"), ("logits", "dve"), ("rank", "dve"), ("gatesT", "dve")])
INDEX = {name: n for n, (name, _) in enumerate(PRODUCTS)}
ORDINAL = {name: sum(e == engine for _, e in PRODUCTS[:n]) for n, (name, engine) in enumerate(PRODUCTS)}
SCORES = [(0, 0, 4), (0, 1, 4), (1, 0, 2), (1, 1, 2), (1, 4, 2), (1, 5, 2)]


def build(nc, x, w_in, w_q_up, w_kv_up, w_ssd_out, w_mla_out, w_o, w_router, w_gate_up, w_down,
          g_mix, conv_w, conv_b, dt_bias, a_log, d_skip, g_ssd_out, g_q_lat, g_kv_lat, g_qk_q, g_qk_k,
          g_ffn, b_router, b_gate_up, b_down, cos, sin, out):
    weights = {"w_in": w_in, "w_q_up": w_q_up, "w_kv_up": w_kv_up, "w_ssd_out": w_ssd_out,
               "w_mla_out": w_mla_out, "w_o": w_o}
    with ExitStack() as ctx:
        def sb(name, shape, dt=F32, where=ctx):
            return where.enter_context(nc.sbuf_tensor(name, shape, dt))

        def sem(name):
            return ctx.enter_context(nc.semaphore(name))

        with ExitStack() as named:
            raw = sb("raw", [P, RAW, SLOT], where=named)
        low = sb("low", [P, RAW, SLOT], F32R)
        resid = sb("resid", [P, TT, D])
        gain_ffn = sb("gain_ffn", [P, D])
        bdown = sb("bdown", [EXPERTS, D])
        wrouter = sb("wrouter", [P, KD, EXPERTS])
        bgu = sb("bgu", [P, EXPERTS, 16])
        ident = sb("ident", [P, P])
        ones = sb("ones", [P, P])
        stacked = sb("stacked", [P, CAP])
        upper = sb("upper", [P, P])
        identb = sb("identb", [P, P], BF16)
        onesb = sb("onesb", [P, P], BF16)
        strictb = sb("strictb", [P, P], BF16)
        causal = sb("causal", [P, P], BF16)
        amask = sb("amask", [P, 2 * P], BF16)
        gmix = sb("gmix", [P, KD])
        cw = sb("cw", [P, XC, CONV])
        cbias = sb("cbias", [P, XC])
        gssd = sb("gssd", [P, KD])
        glat = sb("glat", [P, 5])
        vec16 = sb("vec16", [P, 3, HEADS])
        gq = sb("gq", [P, QK])
        gk = sb("gk", [P, QK])
        brouter = sb("brouter", [P, EXPERTS])
        trig = sb("trig", [P, 2, TT, ROPE // 2])
        stat = sb("stat", [P, 64])
        qkstat = sb("qkstat", [P, 2, TT, AH])
        krsum = sb("krsum", [P, TT])
        sp = sb("sp", [P, 8, TT, HEADS])
        nmax = sb("nmax", [P, 6, 4])
        psums = sb("psums", [P, 6, 4])
        iota_e = sb("iota_e", [P, EXPERTS])
        slot_no = sb("slot_no", [P, P])
        lg = sb("lg", [P, TT, EXPERTS])
        top = sb("top", [P, TT, 8])
        topi = sb("topi", [P, TT, 8], U32)
        topf = sb("topf", [P, TT, 8])
        tg = sb("tg", [P, TT, 8])
        picked = sb("picked", [P, TT, EXPERTS])
        pickedb = sb("pickedb", [P, TT, EXPERTS], BF16)
        gates = sb("gates", [P, TT, EXPERTS + GE])
        gatesT = sb("gatesT", [EXPERTS, TOKENS])
        pos = sb("pos", [P, TT, PASSES * EXPERTS + GE])
        load = sb("load", [P, 4])
        runs_int = sb("runs_int", [P, 1], I32)

        front = ExitStack()
        arena = sb("arena", [P, ARENA], F32, front)
        at = [0]

        def carve(n, start=None):
            a = at[0] if start is None else start
            if start is None:
                at[0] += n
            return arena[:, a:a + n], a

        hT_, hT_at = carve(2048)
        lat_, _ = carve(TT * LAT)
        xc_, xc_at = carve(XC * TOKENS)
        q_, _ = carve(TT * AH * QK)
        kv_, _ = carve(TT * AH * 256)
        gate_, _ = carve(TT * 2 * D)
        zs_, zs_at = carve(TT * D)
        cb_, _ = carve(4 * P)
        A_, A = carve(8228)
        lm_, lm_at = carve(2048)
        y_, y_at = carve(2048)
        btok, _ = carve(2 * P)
        assert at[0] <= ARENA
        hT = hT_.rearrange("p (k t) -> p k t", k=KD)
        yT, oT = hT, hT
        lat = lat_.rearrange("p (t n) -> p t n", t=TT)
        qr = lat[:, :, HEADS:HEADS + AH * ROPE]
        xc = xc_.rearrange("p (c t) -> p c t", c=XC)
        qb = q_.rearrange("p (t h n) -> p t h n", t=TT, h=AH)
        kv = kv_.rearrange("p (t h n) -> p t h n", t=TT, h=AH)
        gate = gate_.rearrange("p (t n) -> p t n", t=TT)
        zs = zs_.rearrange("p (t n) -> p t n", t=TT)
        mT = zs_.rearrange("p (k t) -> p k t", k=KD)
        cb = cb_.rearrange("p (n l) -> p n l", n=4)
        xn = carve(2048, A)[0].rearrange("p (t n) -> p t n", t=TT)
        PADW = TOKENS + CONV - 1
        xbcp = carve(XC * PADW, A + 2048)[0].rearrange("p (c t) -> p c t", c=XC)
        conv = carve(XC * TOKENS, A + 2048 + XC * PADW)[0].rearrange("p (c t) -> p c t", c=XC)
        latent_T = carve(1280, A)[0].rearrange("p (k t) -> p k t", k=5)
        xs = carve(2048, A)[0].rearrange("p (t n) -> p t n", t=TT)
        xdt = carve(2048, A + 2048)[0].rearrange("p (t n) -> p t n", t=TT)
        xdec = carve(1024, A + 4096)[0]
        prev = carve(1024, A + 5120)[0]
        yoff = carve(1024, A + 6144)[0]
        kr = carve(1024, A + 7168)[0].rearrange("p (t h n) -> p t h n", t=TT, h=AH)
        kT = carve(2048, A)[0].rearrange("p (h t) -> p h t", h=AH)
        krT = carve(1024, A + 2048)[0].rearrange("p (h t) -> p h t", h=AH // 2)
        prob = carve(1536, A + 4096)[0].rearrange("p (b n) -> p b n", b=3)
        probT = carve(1536, A + 5632)[0].rearrange("p (b n) -> p b n", b=3)
        qT = carve(2048, xc_at)[0].rearrange("p (h t) -> p h t", h=AH)
        qrT = carve(1024, xc_at + 2048)[0].rearrange("p (h t) -> p h t", h=AH // 2)
        lmat = carve(2048, lm_at)[0].rearrange("p (b h l) -> p b h l", b=4, h=4)
        rope_v = carve(2048, lm_at)[0].rearrange("p (s h n) -> p s h n", s=8, h=AH)
        dump = carve(2048, lm_at)[0].rearrange("p (n c) -> p n c", n=4)
        sq = carve(1536, y_at)[0]
        rope_g = carve(1024, y_at)[0].rearrange("p (s h n) -> p s h n", s=4, h=AH)
        y = y_.rearrange("p (t n) -> p t n", t=TT)
        front.close()

        whi = sb("whi", [P, HIGHS, SLOT], F32R)
        with ExitStack() as named:
            raw_more = sb("raw_more", [P, RING - RAW, SLOT], where=named)
        low_more = sb("low_more", [P, RING - RAW, SLOT], F32R)
        gusb = sb("gusb", [P, 2, D])
        ysb = sb("ysb", [P, 2, D])
        h2hi = sb("h2hi", [P, TT, D], F32R)
        h2lo = sb("h2lo", [P, TT, D], F32R)
        xT = sb("xT", [P, KD, GE, P], F32R)
        actT = sb("actT", [P, KD, P], F32R)
        gu = sb("gu", [P, 8, CAP])
        sg = sb("sg", [P, 4, CAP])
        lin = sb("lin", [P, 4, CAP])
        af = sb("af", [P, 4, CAP])
        pick = sb("pick", [P, TT, GE * CAP], F32R)
        give = sb("give", [P, GE, TT, P])
        giveT = sb("giveT", [P, GE, TOKENS])
        posl = sb("posl", [P, TT, GE])
        gatel = sb("gatel", [P, TT, GE])
        h2 = gusb
        onehot = give[:, 0, :, :].rearrange("p t (k e) -> p t k e", k=TOPK)
        h2T = ysb[:, :, :].rearrange("p a (k t) -> p (a k) t", t=TOKENS)

        ps = [ctx.enter_context(nc.psum_tensor(f"bank{n}", [P, 512], F32)) for n in range(2)]
        ps2 = ctx.enter_context(nc.psum_tensor("bank23", [P, 2, 512], F32))
        psy = ctx.enter_context(nc.psum_tensor("bank45", [P, 2, 512], F32))
        pst = ctx.enter_context(nc.psum_tensor("bank6", [P, 512], F32))
        psm = ctx.enter_context(nc.psum_tensor("bank7", [P, 512], F32))
        banks = [ps[0][:, :], ps[1][:, :], ps2[:, 0, :], ps2[:, 1, :], psy[:, 0, :], psy[:, 1, :],
                 pst[:, :], psm[:, :]]

        def bank(name):
            return banks[INDEX[name] % 8]

        def sc_bank(p, last=False):
            return (ps[0], ps[1], psm, pst if last else psm)[p][:, :]

        x_in = [sem(f"x_in{t}") for t in range(TT)]
        gmix_in = sem("gmix_in")
        small_in = sem("small_in")
        late_in = sem("late_in")
        raw_in = [sem(f"raw_in{r}") for r in range(RING)]
        filled = sem("filled")
        emptied = {"act": sem("emptied_act"), "dve": sem("emptied_dve")}
        consts = sem("consts")
        dve_step = sem("dve_step")
        act_step = sem("act_step")
        pool_step = sem("pool_step")
        one = sem("one")
        x_sq = sem("x_sq")
        x_ms = sem("x_ms")
        x_rt = sem("x_rt")
        xn_done = sem("xn_done")
        lat_sq = sem("lat_sq")
        lat_ms = sem("lat_ms")
        lat_rt = sem("lat_rt")
        lat_done = sem("lat_done")
        dt_raw = sem("dt_raw")
        dt_exp = sem("dt_exp")
        dt_one = sem("dt_one")
        dt_ln = sem("dt_ln")
        dt_done = sem("dt_done")
        padded = sem("padded")
        conv_done = sem("conv_done")
        silu_done = sem("silu_done")
        sq_ready = sem("sq_ready")
        sq_read = sem("sq_read")
        qk_ms = sem("qk_ms")
        qk_rt = sem("qk_rt")
        qk_inv = sem("qk_inv")
        q_done = sem("q_done")
        k_done = sem("k_done")
        decay_done = sem("decay_done")
        xdt_done = sem("xdt_done")
        mmat_done = sem("mmat_done")
        xskip_done = sem("xskip_done")
        yz_done = sem("yz_done")
        y_sq = sem("y_sq")
        y_ms = sem("y_ms")
        y_rt = sem("y_rt")
        yn_done = sem("yn_done")
        max_done = sem("max_done")
        prob_done = sem("prob_done")
        merged = sem("merged")
        x2_sq = sem("x2_sq")
        x2_ms = sem("x2_ms")
        x2_rt = sem("x2_rt")
        h2_done = sem("h2_done")
        h2_split = sem("h2_split")
        top_done = sem("top_done")
        top_exp = sem("top_exp")
        picked_done = sem("picked_done")
        gates_done = sem("gates_done")
        routed = sem("routed")
        w_free = sem("w_free")
        lo_done = sem("lo_done_dve")
        lo_done_pool = sem("lo_done_pool")
        hi_done = sem("hi_done")
        gu_out = sem("gu_out")
        t_filled = sem("t_filled")
        t_read = sem("t_read")
        glu_done = sem("glu_done")
        sig_done = sem("sig_done")
        lin_done = sem("lin_done")
        prod_done = sem("prod_done")
        af_done = sem("af_done")
        ahi_done = sem("ahi_done")
        act_ready = sem("act_ready")
        y_out = sem("y_out")
        sc_filled = sem("sc_filled")
        y_added = sem("y_added")
        pick_ready = sem("pick_ready")
        give_ready = sem("give_ready")
        g_filled = sem("g_filled")
        g_out = sem("g_out")
        x_filled = sem("x_filled")
        x_out = sem("x_out")
        posl_done = sem("posl_done")
        zeroed = sem("zeroed")
        stored = sem("stored")

        def product(eng, name):
            eng.wait_ge(filled, INDEX[name] + 1)
            return bank(name)

        def raw_in_count(n):
            return 16 * (n // RAW + 1)

        def front_slot(n):
            _, _, kk, _, cols, _ = FRONT_SLOTS[n]
            return raw[:, n % RAW, 0:kk * cols].rearrange("p (k n) -> p k n", k=kk)

        def nth(i, j, last=False):
            return HALF + EJ * i + j - (HALF if last else 0) if i >= 0 else j - 6

        def ring_slot(n):
            n %= RING
            return raw[:, n, :] if n < RAW else raw_more[:, n - RAW, :]

        def low_slot(n):
            n %= RING
            return low[:, n, :] if n < RAW else low_more[:, n - RAW, :]

        def high_slot(n):
            return whi[:, n % HIGHS, :]

        def low_order(places, first, G, i, j):
            if i < 0:
                return sum(p in places for p in range(6, j + 1))
            return G * (GE * len(places)) + first + len(places) * i + places.index(j) + 1

        block = ctx.enter_context(nc.Block())

        @block.sync
        def _(sp_):
            for t in range(TT):
                sp_.dma_start(resid[:, t, :], x[P * t:P * t + P, :]).then_inc(x_in[t], 16)
            for n, (name, k0, kk, c0, cols, _) in enumerate(FRONT_SLOTS):
                if n >= RAW:
                    sp_.wait_ge(filled, INDEX[FRONT_SLOTS[n - RAW][5]] + 1)
                src = weights[name].rearrange("(k p) n -> p k n", p=P)[:, k0:k0 + kk, c0:c0 + cols]
                sp_.dma_start(front_slot(n), src).then_inc(raw_in[n % RAW], 16)

            def load_slot(e, n):
                i, j = (n - HALF) // EJ, (n - HALF) % EJ
                if n < HALF:
                    src = w_gate_up[e, n]
                elif i == GE - 1 and j in range(6, 10):
                    src = w_gate_up[next_of(e), j - 6]
                elif j < 4:
                    src = w_gate_up[e + i, HALF + j]
                elif 6 <= j < 10:
                    src = w_gate_up[e + i + 1, j - 6]
                else:
                    src = w_down[e + i, j - 4 if j < 6 else j - 8]
                sp_.dma_start(ring_slot(n), src).then_inc(raw_in[n % RING], 16)

            def next_of(e):
                return 0 if isinstance(e, int) and e == EXPERTS - GE else e + GE

            def rest_of_group(G, e, ns=range(RING, HALF + GE * EJ)):
                for n in ns:
                    sp_.wait_ge(w_free, G * (GE * EJ) + n + 1)
                    load_slot(e, n)

            def start_of_group(G, e):
                for n in range(HALF, RING):
                    sp_.wait_ge(w_free, G * (GE * EJ) + n + 1)
                    load_slot(e, n)

            sp_.wait_ge(filled, INDEX["wo3"] + 1)
            for n in range(RING):
                load_slot(0, n)
            sp_.wait_ge(routed, 1)
            runs = sp_.value_load(runs_int[0:1, 0:1], min_val=0, max_val=PASSES * EXPERTS)
            with sp_.Fori(0, PASSES) as b:
                with sp_.If(runs > b * EXPERTS):
                    with sp_.Fori(0, NG - 1) as g:
                        rest_of_group(b * NG + g, g * GE)
                        start_of_group(b * NG + g + 1, g * GE + GE)
                    G, e, skipped = b * NG + NG - 1, EXPERTS - GE, nth(GE - 1, 6)
                    rest_of_group(G, e, range(RING, skipped))
                    with sp_.If(runs > b * EXPERTS + EXPERTS):
                        rest_of_group(G, e, range(skipped, HALF + GE * EJ))
                        start_of_group(b * NG + NG, 0)
                    with sp_.Else():
                        for j in (10, 11):
                            n = nth(GE - 1, j, last=True)
                            sp_.wait_ge(w_free, G * (GE * EJ) + n + 1)
                            sp_.dma_start(ring_slot(n), w_down[EXPERTS - 1, j - 8]).then_inc(raw_in[n % RING], 16)
            for t in range(TT):
                sp_.wait_ge(y_added, runs * 2 + 2 * t + 2)
                sp_.dma_start(out[P * t:P * t + P, :], resid[:, t, :]).then_inc(stored, 16)
            sp_.wait_ge(stored, 16 * TT)

        @block.gpsimd
        def _(pool):
            steps = [0]

            def settle(ins):
                steps[0] += 1
                ins.then_inc(pool_step, 1)
                pool.wait_ge(pool_step, steps[0])

            for t_, v in ((ident, 0.0), (ones, 1.0), (stacked, 0.0), (upper, 1.0), (identb, 0.0),
                          (onesb, 1.0), (strictb, 1.0), (causal, 0.0), (amask, 0.0)):
                settle(pool.memset(t_[:, :], v))
            diag = [[-1, P]]
            settle(pool.affine_select(out=ident[:, :], in_=ident[:, :], compare_op=ALU.not_equal, fill=1.0,
                                      base=0, pattern=diag, channel_multiplier=1))
            settle(pool.affine_select(out=identb[:, :], in_=identb[:, :], compare_op=ALU.not_equal, fill=1.0,
                                      base=0, pattern=diag, channel_multiplier=1))
            for base in (0, -CAP):
                settle(pool.affine_select(out=stacked[:, :], in_=stacked[:, :], compare_op=ALU.not_equal,
                                          fill=1.0, base=base, pattern=[[-1, CAP]], channel_multiplier=1))
            settle(pool.affine_select(out=upper[:, :], in_=upper[:, :], compare_op=ALU.is_ge, fill=0.0,
                                      base=0, pattern=[[1, P]], channel_multiplier=-1))
            settle(pool.affine_select(out=strictb[:, :], in_=strictb[:, :], compare_op=ALU.is_gt, fill=0.0,
                                      base=0, pattern=[[1, P]], channel_multiplier=-1))
            settle(pool.affine_select(out=causal[:, :], in_=causal[:, :], compare_op=ALU.is_ge, fill=NEG,
                                      base=0, pattern=[[1, P]], channel_multiplier=-1))
            settle(pool.affine_select(out=amask[:, P + CHUNK:2 * P], in_=amask[:, P + CHUNK:2 * P], compare_op=ALU.is_ge,
                                      fill=NEG, base=-CHUNK, pattern=[[0, P - CHUNK]], channel_multiplier=1))
            settle(pool.iota(iota_e[:, :], pattern=[[1, EXPERTS]], base=0, channel_multiplier=0,
                             allow_small_or_imprecise_dtypes=True))
            pool.iota(slot_no[:, :].rearrange("p (a n) -> p a n", a=2), pattern=[[0, 2], [1, CAP]], base=0,
                      channel_multiplier=0, allow_small_or_imprecise_dtypes=True).then_inc(consts, 1)
            pool.memset(xbcp[:, :, 0:CONV - 1], 0.0).then_inc(padded, 1)

            n = 0
            for t in range(TT):
                pool.wait_ge(emptied["act"], ORDINAL["qup5"] + 1)
                if n:
                    pool.wait_ge(sq_read, n)
                pool.tensor_tensor(sq[:, 0:AH * QK].rearrange("p (h n) -> p h n", h=AH), qb[:, t], qb[:, t],
                                   ALU.mult).then_inc(sq_ready, 1)
                n += 1
            for t in range(TT):
                pool.wait_ge(emptied["act"], ORDINAL["kvup7"] + 1)
                pool.wait_ge(sq_read, n)
                pool.tensor_tensor(sq[:, 0:AH * NOPE].rearrange("p (h n) -> p h n", h=AH),
                                   kv[:, t, :, 0:NOPE], kv[:, t, :, 0:NOPE], ALU.mult).then_inc(sq_ready, 1)
                n += 1
            pool.wait_ge(sq_read, n)
            pool.wait_ge(qk_inv, 1)
            pool.wait_ge(silu_done, 3)
            for t in range(TT):
                inv = qkstat[:, 1, t, :]
                kn = kv[:, t, :, 0:NOPE]
                settle(pool.tensor_tensor(kn, kn, inv.unsqueeze(2).to_broadcast([P, AH, NOPE]), ALU.mult))
                settle(pool.tensor_tensor(kn, kn, gk[:, 0:NOPE].unsqueeze(1).to_broadcast([P, AH, NOPE]), ALU.mult))
                krow = lat[:, t, LAT - ROPE:LAT].unsqueeze(1).to_broadcast([P, AH, ROPE])
                settle(pool.tensor_tensor(kr[:, t], krow, inv.unsqueeze(2).to_broadcast([P, AH, ROPE]), ALU.mult))
                settle(pool.tensor_tensor(kr[:, t], kr[:, t], gk[:, NOPE:QK].unsqueeze(1).to_broadcast([P, AH, ROPE]), ALU.mult))
                c = trig[:, 0, t, :].unsqueeze(1).to_broadcast([P, AH, ROPE // 2])
                s = trig[:, 1, t, :].unsqueeze(1).to_broadcast([P, AH, ROPE // 2])
                k1, k2 = kr[:, t, :, 0:ROPE // 2], kr[:, t, :, ROPE // 2:ROPE]
                pool.tensor_tensor(rope_g[:, 0], k1, c, ALU.mult)
                pool.tensor_tensor(rope_g[:, 1], k2, s, ALU.mult)
                pool.tensor_tensor(rope_g[:, 2], k2, c, ALU.mult)
                settle(pool.tensor_tensor(rope_g[:, 3], k1, s, ALU.mult))
                settle(pool.tensor_tensor(k1, rope_g[:, 0], rope_g[:, 1], ALU.subtract))
                ins = pool.tensor_tensor(k2, rope_g[:, 2], rope_g[:, 3], ALU.add)
                ins.then_inc(k_done, 1)
                pool.wait_ge(k_done, t + 1)
            pool.wait_ge(emptied["act"], ORDINAL["xsT3"] + 1)
            pool.wait_ge(dt_done, 1)
            for t in range(TT):
                xh = xs[:, t, :].rearrange("p (h n) -> p h n", h=HEADS)
                settle(pool.tensor_tensor(xdt[:, t, :].rearrange("p (h n) -> p h n", h=HEADS), xh,
                                          sp[:, 0, t, :].unsqueeze(2).to_broadcast([P, HEADS, HD]), ALU.mult))
            pool.wait_ge(decay_done, 2)
            pool.tensor_tensor(xdec.rearrange("p (h n) -> p h n", h=HEADS),
                               xdt[:, 0, :].rearrange("p (h n) -> p h n", h=HEADS),
                               sp[:, 3, 0, :].unsqueeze(2).to_broadcast([P, HEADS, HD]), ALU.mult).then_inc(xdt_done, 1)
            for t in range(TT):
                xh = xs[:, t, :].rearrange("p (h n) -> p h n", h=HEADS)
                pool.tensor_tensor(xh, xh, vec16[:, 2, :].unsqueeze(2).to_broadcast([P, HEADS, HD]),
                                   ALU.mult).then_inc(xskip_done, 1)

            def localise(column, column_g):
                pool.tensor_copy(posl[:, :, :], pos[:, :, column:column + GE] if isinstance(column, int)
                                 else pos[:, :, bass.ds(column, GE)])
                pool.tensor_copy(gatel[:, :, :], gates[:, :, column_g:column_g + GE] if isinstance(column_g, int)
                                 else gates[:, :, bass.ds(column_g, GE)]).then_inc(posl_done, 1)

            def pick_tokens():
                for t in range(TT):
                    for i in range(GE):
                        ins = pool.tensor_scalar(pick[:, t, CAP * i:CAP * i + CAP], slot_no[:, 0:CAP],
                                                 posl[:, t, i:i + 1], None, ALU.is_equal)
                ins.then_inc(pick_ready, 1)

            def give_gates(i):
                for t in range(TT):
                    ins = pool.tensor_scalar(give[:, i, t, :], slot_no[:, :], posl[:, t, i:i + 1],
                                             gatel[:, t, i:i + 1], ALU.is_equal, ALU.mult)
                ins.then_inc(give_ready, 1)

            def low_part(G, i, j):
                n = nth(i, j)
                pool.wait_ge(hi_done, G * (GE * EJ) + n + 1)
                pool.tensor_tensor(low_slot(n), ring_slot(n), high_slot(n).bitcast(F32),
                                   ALU.subtract).then_inc(lo_done_pool, 1)

            pool.wait_ge(w_free, RING)
            for j in POOL_PLACES:
                if j in range(6, 10):
                    low_part(0, -1, j)
            pool.memset(giveT[:, :, :], 0.0).then_inc(zeroed, 1)
            pool.wait_ge(filled, INDEX["logitsT"] + 1)
            pool.memset(ysb[:, :, :], 0.0).then_inc(zeroed, 1)
            pool.wait_ge(routed, 1)
            runs = pool.value_load(runs_int[0:1, 0:1], min_val=0, max_val=PASSES * EXPERTS)
            localise(0, 0)
            pool.wait_ge(posl_done, 1)
            for i in range(GE):
                give_gates(i)

            def turn(G, i, g, last=False):
                if i == 0:
                    pool.wait_ge(x_filled, G * KD + KD)
                    pool.wait_ge(give_ready, G * GE + GE)
                low_part(G, i, POOL_PLACES[0])
                if i == 0:
                    localise(G * GE + GE, g * GE + GE)
                    pool.wait_ge(posl_done, G + 2)
                if not last:
                    pool.wait_ge(g_filled, G * GE + i + 1)
                    low_part(G, i, POOL_PLACES[1])
                    if i == 0:
                        pick_tokens()
                    give_gates(i)

            with pool.Fori(0, PASSES) as b:
                with pool.If(runs > b * EXPERTS):
                    with pool.Fori(0, NG) as g:
                        G = b * NG + g
                        for i in range(GE - 1):
                            turn(G, i, g)
                        with pool.If(runs > G * GE + GE):
                            turn(G, GE - 1, g)
                        with pool.Else():
                            turn(G, GE - 1, g, last=True)

        @block.scalar
        def _(act):
            steps = [0]

            def settle(ins):
                steps[0] += 1
                ins.then_inc(act_step, 1)
                act.wait_ge(act_step, steps[0])

            def load_small(pairs, done):
                for dst, src in pairs:
                    act.dma_start(dst, src).then_inc(done, 16)

            def want_sqrt():
                act.activation(stat[:, 59:60], stat[:, 58:59], ACT.Sqrt)

            load_small(((gmix[:, :], g_mix),), gmix_in)
            act.wait_ge(one, 1)
            want_sqrt()
            load_small(((vec16[:, 0, :], dt_bias), (vec16[:, 1, :], a_log)), small_in)
            for t in range(TT):
                act.wait_ge(x_in[t], 16)
                act.activation(xn[:, t, :], resid[:, t, :], ACT.Square, accum_out=stat[:, t:t + 1]).then_inc(x_sq, 1)
            act.wait_ge(x_ms, 1)
            act.activation(stat[:, 2:4], stat[:, 2:4], ACT.Sqrt).then_inc(x_rt, 1)
            load_small(((vec16[:, 2, :], d_skip), (glat[:, 0:3], g_q_lat), (glat[:, 3:5], g_kv_lat),
                        (cw[:, :, :], conv_w), (cbias[:, :], conv_b), (gssd[:, :], g_ssd_out), (gq[:, :], g_qk_q),
                        (gk[:, :], g_qk_k), (trig[:, 0, :, :], cos), (trig[:, 1, :, :], sin)), small_in)
            load_small(((gain_ffn[:, :], g_ffn), (bdown[:, :], b_down), (wrouter[:, :, :], w_router),
                        (bgu[:, :, :], b_gate_up), (brouter[:, :], b_router)), late_in)

            for n in range(4):
                t, part = n % 2, n // 2
                src = product(act, f"lat{n}")
                a, cols = (0, CA) if part == 0 else (CA, CB_)
                act.activation(lat[:, t, a:a + cols], src[:, 0:cols], ACT.Copy).then_inc(emptied["act"], 1)
            act.wait_ge(emptied["act"], ORDINAL["lat3"] + 1)
            act.wait_ge(xn_done, TT)
            act.wait_ge(filled, INDEX["hT3"] + 1)
            for t in range(TT):
                act.activation(xn[:, t, 0:QR], lat[:, t, HEADS:CA], ACT.Square,
                               accum_out=stat[:, 4 + t:5 + t]).then_inc(lat_sq, 1)
                act.activation(xn[:, t, 512:512 + KVR], lat[:, t, CA:CA + KVR], ACT.Square,
                               accum_out=stat[:, 6 + t:7 + t]).then_inc(lat_sq, 1)
                act.activation(xn[:, t, 800:800 + ROPE], lat[:, t, LAT - ROPE:LAT], ACT.Square,
                               accum_out=krsum[:, t:t + 1]).then_inc(lat_sq, 1)
            act.wait_ge(lat_ms, 1)
            act.activation(stat[:, 8:12], stat[:, 8:12], ACT.Sqrt).then_inc(lat_rt, 1)
            act.wait_ge(dt_raw, 1)
            settle(act.activation(sp[:, 2, :, :], sp[:, 1, :, :], ACT.Abs))
            act.activation(sp[:, 2, :, :], sp[:, 2, :, :], ACT.Exp, scale=-1.0).then_inc(dt_exp, 1)
            act.wait_ge(small_in, 12 * 16)
            act.activation(vec16[:, 1, :], vec16[:, 1, :], ACT.Exp).then_inc(dt_exp, 1)
            act.wait_ge(dt_one, 1)
            act.activation(sp[:, 4, :, :], sp[:, 3, :, :], ACT.Ln).then_inc(dt_ln, 1)
            act.wait_ge(padded, 1)
            for n in range(6):
                src = product(act, f"xbc{n}").rearrange("p (c t) -> p c t", c=2)
                act.activation(xbcp[:, 2 * n:2 * n + 2, CONV - 1:PADW], src, ACT.Copy).then_inc(emptied["act"], 1)
            for n in range(4):
                t, s = n % 2, n // 2
                act.activation(zs[:, t, 512 * s:512 * s + 512], product(act, f"z{n}"), ACT.Silu).then_inc(emptied["act"], 1)
            for n in range(3):
                act.wait_ge(conv_done, 4 * n + 4)
                act.activation(xc[:, 4 * n:4 * n + 4, :], conv[:, 4 * n:4 * n + 4, :], ACT.Silu).then_inc(silu_done, 1)
            for n in range(6):
                t, s = n % 2, n // 2
                act.activation(qb[:, t].rearrange("p h n -> p (h n)")[:, 512 * s:512 * s + 512],
                               product(act, f"qup{n}"), ACT.Copy).then_inc(emptied["act"], 1)
            for n in range(8):
                t, s = n % 2, n // 2
                act.activation(kv[:, t].rearrange("p h n -> p (h n)")[:, 512 * s:512 * s + 512],
                               product(act, f"kvup{n}"), ACT.Copy).then_inc(emptied["act"], 1)
            act.wait_ge(qk_ms, 1)
            act.activation(qkstat[:, :, :, :], qkstat[:, :, :, :], ACT.Sqrt).then_inc(qk_rt, 1)
            def merge_gate(n):
                t, s = n % 2, n // 2
                act.activation(gate[:, t, 512 * s:512 * s + 512], product(act, f"gate{n}"), ACT.Sigmoid).then_inc(emptied["act"], 1)

            for n in range(6):
                merge_gate(n)
            act.wait_ge(silu_done, 3)
            for n in range(4):
                t, h = n % 2, n // 2
                act.activation(xs[:, t, 512 * h:512 * h + 512], product(act, f"xsT{n}"), ACT.Copy).then_inc(emptied["act"], 1)
            act.wait_ge(emptied["dve"], ORDINAL["acum"] + 1)
            act.activation(sp[:, 3, 0, :], sp[:, 7, 0, :], ACT.Exp).then_inc(decay_done, 1)
            act.activation(sp[:, 3, 1, :], sp[:, 6, 1, :], ACT.Exp, scale=-1.0).then_inc(decay_done, 1)
            for n in range(8):
                t = n // 4
                src = product(act, f"acumb{n}")
                if n >= 4:
                    act.wait_ge(filled, INDEX[f"ydiag{(n - 4) // 2}"] + 1)
                for hh in range(4):
                    h = 4 * (n % 4) + hh
                    ins = act.activation(lmat[:, n % 4, hh, :], src[:, P * hh:P * hh + P], ACT.Exp,
                                         bias=sp[:, 6, t, h:h + 1])
                    if hh == 3:
                        ins.then_inc(emptied["act"], 1)
            act.wait_ge(filled, INDEX["ydiag3"] + 1)
            for n in range(6):
                src = product(act, f"qT{n}").rearrange("p (h t) -> p h t", h=4)
                t, part = n % 2, n // 2
                dst = (qT[:, 4 * part:4 * part + 4, P * t:P * t + P] if part < 2 else
                       qrT[:, :, P * t:P * t + P])
                act.activation(dst, src, ACT.Copy).then_inc(emptied["act"], 1)
            want_sqrt()
            act.wait_ge(yz_done, 2)
            for t in range(TT):
                for g in range(GROUPS):
                    act.activation(dump[:, 2 * t + g, :], y[:, t, 512 * g:512 * g + 512], ACT.Square,
                                   accum_out=stat[:, 12 + 2 * t + g:13 + 2 * t + g]).then_inc(y_sq, 1)
            act.wait_ge(y_ms, 1)
            act.activation(stat[:, 16:20], stat[:, 16:20], ACT.Sqrt).then_inc(y_rt, 1)
            for n in range(6):
                src = product(act, f"kT{n}").rearrange("p (h t) -> p h t", h=4)
                t, part = n % 2, n // 2
                dst = (kT[:, 4 * part:4 * part + 4, P * t:P * t + P] if part < 2 else
                       krT[:, :, P * t:P * t + P])
                act.activation(dst, src, ACT.Copy).then_inc(emptied["act"], 1)

            merge_gate(6)
            merge_gate(7)

            def softmax_exp(n):
                j, _, hs = SCORES[n]
                keys = P * (j + 1)
                src = product(act, f"S{n}")
                act.wait_ge(max_done, n + 1)
                if n >= 3:
                    act.wait_ge(filled, INDEX[f"PT{n - 3}"] + 1)
                for h in range(hs):
                    ins = act.activation(prob[:, n % 3, keys * h:keys * h + keys], src[:, keys * h:keys * h + keys],
                                         ACT.Exp, bias=nmax[:, n, h:h + 1], scale=SCALE,
                                         accum_out=psums[:, n, h:h + 1])
                ins.then_inc(emptied["act"], 1)

            def probs_by_key(n):
                src = product(act, f"PT{n}")
                if n >= 3:
                    act.wait_ge(filled, INDEX[f"O{n - 3}"] + 1)
                act.activation(probT[:, n % 3, :], src, ACT.Copy).then_inc(emptied["act"], 1)

            for name, who in PRODUCTS[INDEX["S0"]:INDEX["O5"] + 1]:
                if who == "act":
                    (softmax_exp if name[0] == "S" else probs_by_key)(int(name[-1]))
            for n in range(4):
                t, h = n % 2, n // 2
                src = product(act, f"mT{n}").rearrange("p (k t) -> p k t", k=4)
                act.activation(mT[:, 4 * h:4 * h + 4, P * t:P * t + P], src, ACT.Copy).then_inc(emptied["act"], 1)
            def gathered(k, G, gather_bank=psm):
                act.wait_ge(x_filled, G * KD + k + 1)
                src = gather_bank[:, :].rearrange("p (part i s) -> p part i s", part=2, i=GE)
                dst = xT[:, k, :, :].rearrange("p i (part s) -> p part i s", part=2)
                for part in range(2):
                    ins = act.activation(dst[:, part], src[:, part], ACT.Copy)
                ins.then_inc(x_out, 1)

            def high_part(G, i, j, last=False):
                n = nth(i, j, last)
                before = sum(1 for m in range(NF) if m % RAW == n % RING)
                act.wait_ge(raw_in[n % RING], G * (GE * EJ // RING * 16) + 16 * (before + n // RING + 1))
                act.wait_ge(w_free, G * (GE * EJ) + n + RING - HIGHS + 1)
                act.activation(high_slot(n), ring_slot(n), ACT.Copy).then_inc(hi_done, 1)

            def sums_out(G, i, hf):
                used = nth(i, 3) + 1 if hf else nth(i - 1, 9) + 1 if i else HALF
                act.wait_ge(w_free, G * (GE * EJ) + used + RING)
                for s in range(2):
                    src = ps[s][:, :] if hf == 0 else ps2[:, s, :]
                    act.activation(gusb[:, hf, 512 * s:512 * s + 512], src, ACT.Copy).then_inc(gu_out, 1)

            def sigmoid(G, i, hf):
                act.wait_ge(glu_done, G * (2 * GE) + 2 * i + hf + 1)
                act.activation(sg[:, :, :], gu[:, 0:4, :], ACT.Sigmoid, scale=ALPHA).then_inc(sig_done, 1)

            def outputs_out(E, i, last=False):
                act.wait_ge(w_free, E * EJ + (0 if last else HALF) + RING)
                act.activation(ysb[:, (i - 1) % 2, :].rearrange("p (a n) -> p a n", a=2), psy[:, :, :],
                               ACT.Copy).then_inc(y_out, 1)

            want_sqrt()
            for t in range(TT):
                act.wait_ge(emptied["dve"], ORDINAL[f"wo{2 + t}"] + 1)
                act.activation(h2[:, t, :], resid[:, t, :], ACT.Square, accum_out=stat[:, 20 + t:21 + t]).then_inc(x2_sq, 1)
            act.wait_ge(x2_ms, 1)
            act.activation(stat[:, 22:24], stat[:, 22:24], ACT.Sqrt).then_inc(x2_rt, 1)
            for n in range(4):
                t, h = n % 2, n // 2
                src = product(act, f"h2T{n}").rearrange("p (k t) -> p k t", k=4)
                act.activation(h2T[:, 4 * h:4 * h + 4, P * t:P * t + P], src, ACT.Copy).then_inc(emptied["act"], 1)
            for j in range(6, 10):
                high_part(0, -1, j)
            act.wait_ge(top_done, 2)
            for t in range(TT):
                act.activation(tg[:, t, 0:4], top[:, t, 0:4], ACT.Exp, bias=tg[:, t, 4:5],
                               accum_out=tg[:, t, 5:6]).then_inc(top_exp, 1)

            for k in range(KD):
                gathered(k, 0, (psm, pst)[k % 2])
            act.wait_ge(routed, 1)
            runs = act.value_load(runs_int[0:1, 0:1], min_val=0, max_val=PASSES * EXPERTS)
            def turn(G, i, last=False):
                E = G * GE + i
                gathers = i == GE - 1 and not last
                high_part(G, i, 0)
                sums_out(G, i, 0)
                for j in (1, 2, 3):
                    high_part(G, i, j)
                act.wait_ge(g_filled, E + 1)
                act.activation(giveT[:, i, :], psm[:, 0:TOKENS], ACT.Copy).then_inc(g_out, 1)
                if gathers:
                    gathered(0, G + 1)
                if i == 0:
                    act.wait_ge(zeroed, 3)
                if i % 2:
                    act.wait_ge(sc_filled, 2 * E + 2)
                outputs_out(E, i)
                high_part(G, i, 4)
                if gathers:
                    gathered(1, G + 1)
                    gathered(2, G + 1)
                high_part(G, i, 5)
                if gathers:
                    gathered(3, G + 1)
                    gathered(4, G + 1)
                sigmoid(G, i, 0)
                if not last:
                    high_part(G, i, 6)
                if gathers:
                    gathered(5, G + 1)
                    gathered(6, G + 1)
                sums_out(G, i, 1)
                if not last:
                    high_part(G, i, 7)
                if gathers:
                    gathered(7, G + 1)
                if not last:
                    high_part(G, i, 8)
                    high_part(G, i, 9)
                high_part(G, i, 10, last)
                if last:
                    high_part(G, i, 11, last)
                    sigmoid(G, i, 1)
                else:
                    sigmoid(G, i, 1)
                    high_part(G, i, 11)

            with act.Fori(0, PASSES) as b:
                with act.If(runs > b * EXPERTS):
                    with act.Fori(0, NG) as g:
                        G = b * NG + g
                        for i in range(GE - 1):
                            turn(G, i)
                        with act.If(runs > G * GE + GE):
                            turn(G, GE - 1)
                        with act.Else():
                            turn(G, GE - 1, last=True)
            outputs_out(runs, 0, last=True)

        @block.vector
        def _(dve):
            steps = [0]

            def settle(ins):
                steps[0] += 1
                ins.then_inc(dve_step, 1)
                dve.wait_ge(dve_step, steps[0])

            def mean_eps(a, b, n, done):
                dve.tensor_scalar(stat[:, b], stat[:, a], 1.0 / n, EPS, ALU.mult, ALU.add).then_inc(done, 1)

            dve.memset(stat[:, 58:59], 1.0).then_inc(one, 1)
            dve.wait_ge(x_sq, TT)
            mean_eps(slice(0, 2), slice(2, 4), D, x_ms)
            dve.wait_ge(x_rt, 1)
            settle(dve.reciprocal(stat[:, 2:4], stat[:, 2:4]))
            for t in range(TT):
                dve.tensor_scalar(xn[:, t, :], resid[:, t, :], stat[:, 2 + t:3 + t], None, ALU.mult).then_inc(xn_done, 1)
            dve.wait_ge(gmix_in, 16)
            for n in range(4):
                t, h = n % 2, n // 2
                src = product(dve, f"hT{n}").rearrange("p (k t) -> p k t", k=4)
                dve.tensor_tensor(hT[:, 4 * h:4 * h + 4, P * t:P * t + P], src,
                                  gmix[:, 4 * h:4 * h + 4].unsqueeze(2).to_broadcast([P, 4, P]),
                                  ALU.mult).then_inc(emptied["dve"], 1)
            dve.wait_ge(small_in, 12 * 16)
            dve.wait_ge(emptied["act"], ORDINAL["lat3"] + 1)
            dve.tensor_tensor(sp[:, 1, :, :], lat[:, :, 0:HEADS], vec16[:, 0, :].unsqueeze(1).to_broadcast([P, TT, HEADS]),
                              ALU.add).then_inc(dt_raw, 1)
            dve.wait_ge(lat_sq, 3 * TT)
            settle(dve.tensor_scalar(stat[:, 8:10], stat[:, 4:6], 1.0 / QR, EPS, ALU.mult, ALU.add))
            mean_eps(slice(6, 8), slice(10, 12), KVR, lat_ms)
            dve.wait_ge(lat_rt, 1)
            settle(dve.reciprocal(stat[:, 8:12], stat[:, 8:12]))
            for t in range(TT):
                dve.tensor_scalar(lat[:, t, HEADS:CA], lat[:, t, HEADS:CA], stat[:, 8 + t:9 + t], None, ALU.mult).then_inc(lat_done, 1)
                dve.tensor_scalar(lat[:, t, CA:CA + KVR], lat[:, t, CA:CA + KVR], stat[:, 10 + t:11 + t], None, ALU.mult).then_inc(lat_done, 1)
            dve.wait_ge(dt_exp, 2)
            e_, u_, l_, d_, s_ = (sp[:, n, :, :] for n in (2, 3, 4, 5, 6))
            dve.tensor_scalar(u_, e_, 1.0, None, ALU.add).then_inc(dt_one, 1)
            dve.wait_ge(dt_one, 1)
            settle(dve.tensor_scalar(d_, u_, -1.0, None, ALU.add))
            settle(dve.scalar_tensor_tensor(out=s_, in0=d_, scalar=0.0, in1=e_, op0=ALU.is_equal, op1=ALU.mult))
            settle(dve.tensor_scalar(d_, d_, 1e-30, None, ALU.max))
            settle(dve.reciprocal(d_, d_))
            settle(dve.tensor_tensor(d_, d_, e_, ALU.mult))
            dve.wait_ge(dt_ln, 1)
            settle(dve.tensor_tensor(d_, d_, l_, ALU.mult))
            settle(dve.tensor_tensor(d_, d_, s_, ALU.add))
            settle(dve.scalar_tensor_tensor(out=sp[:, 0, :, :], in0=sp[:, 1, :, :], scalar=0.0, in1=d_, op0=ALU.max, op1=ALU.add))
            dve.scalar_tensor_tensor(out=sp[:, 5, :, :], in0=sp[:, 0, :, :], scalar=-1.0,
                                     in1=vec16[:, 1, :].unsqueeze(1).to_broadcast([P, TT, HEADS]),
                                     op0=ALU.mult, op1=ALU.mult).then_inc(dt_done, 1)
            for c in range(XC):
                dve.wait_ge(emptied["act"], ORDINAL[f"xbc{c // 2}"] + 1)
                settle(dve.tensor_scalar(conv[:, c, :], xbcp[:, c, 0:TOKENS], cw[:, c, 0:1], cbias[:, c:c + 1], ALU.mult, ALU.add))
                for w in range(1, CONV):
                    ins = dve.scalar_tensor_tensor(out=conv[:, c, :], in0=xbcp[:, c, w:w + TOKENS], scalar=cw[:, c, w:w + 1],
                                                   in1=conv[:, c, :], op0=ALU.mult, op1=ALU.add)
                    if w < CONV - 1:
                        settle(ins)
                ins.then_inc(conv_done, 1)
            for n in range(4):
                t, part = n % 2, n // 2
                k0, kk = (0, 3) if part == 0 else (3, 2)
                src = product(dve, f"latT{n}")[:, 0:kk * P].rearrange("p (k t) -> p k t", k=kk)
                dve.tensor_tensor(latent_T[:, k0:k0 + kk, P * t:P * t + P], src,
                                  glat[:, k0:k0 + kk].unsqueeze(2).to_broadcast([P, kk, P]),
                                  ALU.mult).then_inc(emptied["dve"], 1)
            for n in range(4):
                which, t = n // 2, n % 2
                width = QK if which == 0 else NOPE
                dve.wait_ge(sq_ready, n + 1)
                dve.tensor_reduce(qkstat[:, which, t, :], sq[:, 0:AH * width].rearrange("p (h n) -> p h n", h=AH),
                                  AX.X, ALU.add).then_inc(sq_read, 1)
            dve.wait_ge(sq_read, 4)
            settle(dve.tensor_tensor(qkstat[:, 1, :, :], qkstat[:, 1, :, :], krsum[:, :].unsqueeze(2).to_broadcast([P, TT, AH]), ALU.add))
            dve.tensor_scalar(qkstat[:, :, :, :], qkstat[:, :, :, :], 1.0 / QK, EPS, ALU.mult, ALU.add).then_inc(qk_ms, 1)
            dve.wait_ge(qk_rt, 1)
            dve.reciprocal(qkstat[:, :, :, :], qkstat[:, :, :, :]).then_inc(qk_inv, 1)
            dve.wait_ge(qk_inv, 1)
            for t in range(TT):
                settle(dve.tensor_tensor(qb[:, t], qb[:, t], qkstat[:, 0, t, :].unsqueeze(2).to_broadcast([P, AH, QK]), ALU.mult))
                settle(dve.tensor_tensor(qb[:, t], qb[:, t], gq[:, :].unsqueeze(1).to_broadcast([P, AH, QK]), ALU.mult))
                c = trig[:, 0, t, :].unsqueeze(1).to_broadcast([P, AH, ROPE // 2])
                s = trig[:, 1, t, :].unsqueeze(1).to_broadcast([P, AH, ROPE // 2])
                q1, q2 = qb[:, t, :, NOPE:NOPE + ROPE // 2], qb[:, t, :, NOPE + ROPE // 2:QK]
                r0 = 4 * t
                dve.tensor_tensor(rope_v[:, r0], q1, c, ALU.mult)
                dve.tensor_tensor(rope_v[:, r0 + 1], q2, s, ALU.mult)
                dve.tensor_tensor(rope_v[:, r0 + 2], q2, c, ALU.mult)
                settle(dve.tensor_tensor(rope_v[:, r0 + 3], q1, s, ALU.mult))
                rot = qr[:, t, :].rearrange("p (h n) -> p h n", h=AH)
                dve.tensor_tensor(rot[:, :, 0:ROPE // 2], rope_v[:, r0], rope_v[:, r0 + 1], ALU.subtract)
                dve.tensor_tensor(rot[:, :, ROPE // 2:ROPE], rope_v[:, r0 + 2], rope_v[:, r0 + 3], ALU.add).then_inc(q_done, 1)
            dve.tensor_copy(btok, product(dve, "btok")[:, 0:2 * P]).then_inc(emptied["dve"], 1)
            dve.tensor_copy(cb_, product(dve, "cb")).then_inc(emptied["dve"], 1)
            src = product(dve, "acum")
            cum = src[:, 0:2 * HEADS].rearrange("p (t h) -> p t h", t=TT)
            settle(dve.tensor_scalar(sp[:, 6, :, :], cum, -1.0, None, ALU.mult))
            dve.tensor_tensor(sp[:, 7, 0, :], src[:, 2 * HEADS:3 * HEADS], sp[:, 6, 0, :], ALU.add).then_inc(emptied["dve"], 1)
            def decayed_product(n):
                t, g = n // 4, (n % 4) // 2
                dve.wait_ge(emptied["act"], ORDINAL[f"acumb{n}"] + 1)
                dve.tensor_tensor(lmat[:, n % 4], lmat[:, n % 4], cb[:, 2 * t + g, :].unsqueeze(1).to_broadcast([P, 4, P]),
                                  ALU.mult).then_inc(mmat_done, 1)

            def state(g):
                dve.tensor_copy(prev[:, 512 * g:512 * g + 512], product(dve, f"state{g}")).then_inc(emptied["dve"], 1)

            def from_state(g):
                src = product(dve, f"yoff{g}").rearrange("p (h n) -> p h n", h=HG)
                dve.wait_ge(decay_done, 2)
                dve.tensor_tensor(yoff[:, 512 * g:512 * g + 512].rearrange("p (h n) -> p h n", h=HG), src,
                                  sp[:, 3, 1, HG * g:HG * g + HG].unsqueeze(2).to_broadcast([P, HG, HD]),
                                  ALU.mult).then_inc(emptied["dve"], 1)

            def ssd_out(n):
                t, g = n // 2, n % 2
                src = product(dve, f"ydiag{n}")
                cols = slice(512 * g, 512 * g + 512)
                dve.wait_ge(xskip_done, 2)
                dve.tensor_tensor(y[:, t, cols], src, xs[:, t, cols], ALU.add).then_inc(emptied["dve"], 1)
                dve.wait_ge(emptied["dve"], ORDINAL[f"ydiag{n}"] + 1)
                if t == 1:
                    settle(dve.tensor_tensor(y[:, t, cols], y[:, t, cols], yoff[:, cols], ALU.add))

            for n in range(4):
                decayed_product(n)
            for g in range(GROUPS):
                state(g)
            for g in range(GROUPS):
                from_state(g)
            ssd_out(0)
            decayed_product(4)
            decayed_product(5)
            ssd_out(1)
            decayed_product(6)
            decayed_product(7)
            ssd_out(2)
            ssd_out(3)
            for t in range(TT):
                dve.tensor_tensor(y[:, t, :], y[:, t, :], zs[:, t, :], ALU.mult).then_inc(yz_done, 1)
            dve.wait_ge(y_sq, 4)
            mean_eps(slice(12, 16), slice(16, 20), 512, y_ms)
            dve.wait_ge(y_rt, 1)
            settle(dve.reciprocal(stat[:, 16:20], stat[:, 16:20]))
            for t in range(TT):
                for g in range(GROUPS):
                    yg = y[:, t, 512 * g:512 * g + 512]
                    dve.tensor_scalar(yg, yg, stat[:, 16 + 2 * t + g:17 + 2 * t + g], None, ALU.mult).then_inc(yn_done, 1)
            for n in range(4):
                t, h = n % 2, n // 2
                src = product(dve, f"yT{n}").rearrange("p (k t) -> p k t", k=4)
                dve.tensor_tensor(yT[:, 4 * h:4 * h + 4, P * t:P * t + P], src,
                                  gssd[:, 4 * h:4 * h + 4].unsqueeze(2).to_broadcast([P, 4, P]),
                                  ALU.mult).then_inc(emptied["dve"], 1)
            def ssd_gated(n):
                t, s = n % 2, n // 2
                cols = slice(512 * s, 512 * s + 512)
                dve.tensor_tensor(y[:, t, cols], product(dve, f"ssdout{n}"), gate[:, t, cols], ALU.mult).then_inc(emptied["dve"], 1)

            def score_max(n):
                j, _, hs = SCORES[n]
                src = product(dve, f"S{n}")[:, 0:hs * P * (j + 1)].rearrange("p (h k) -> p h k", h=hs)
                settle(dve.tensor_reduce(nmax[:, n, 0:hs], src, AX.X, ALU.max))
                dve.tensor_scalar(nmax[:, n, 0:hs], nmax[:, n, 0:hs], -SCALE, None, ALU.mult).then_inc(max_done, 1)

            def normalise(n):
                j, _, hs = SCORES[n]
                dve.wait_ge(emptied["act"], ORDINAL[f"S{n}"] + 1)
                settle(dve.reciprocal(psums[:, n, 0:hs], psums[:, n, 0:hs]))
                pv = prob[:, n % 3, :].rearrange("p (h k) -> p h k", h=hs)
                dve.tensor_tensor(pv, pv, psums[:, n, 0:hs].unsqueeze(2).to_broadcast([P, hs, P * (j + 1)]), ALU.mult).then_inc(prob_done, 1)

            def heads_out(n):
                j, h0, hs = SCORES[n]
                src = product(dve, f"O{n}")[:, 0:hs * P].rearrange("p (h q) -> p h q", h=hs)
                dve.tensor_copy(oT[:, h0:h0 + 2 * hs - 1:2, P * j:P * j + P], src).then_inc(emptied["dve"], 1)

            for name, _ in PRODUCTS[INDEX["S0"]:INDEX["O5"] + 1]:
                n = int(name[-1])
                if name[0] == "S":
                    score_max(n)
                    normalise(n)
                elif name[0] == "O":
                    heads_out(n)
                elif name[0] == "s":
                    ssd_gated(n)
            for n in range(4):
                t, s = n % 2, n // 2
                cols = slice(512 * s, 512 * s + 512)
                src = product(dve, f"mlaout{n}")
                gcols = gate[:, t, D + 512 * s:D + 512 * s + 512]
                dve.tensor_tensor(gcols, src, gcols, ALU.mult).then_inc(emptied["dve"], 1)
                dve.wait_ge(emptied["dve"], ORDINAL[f"mlaout{n}"] + 1)
                dve.tensor_tensor(y[:, t, cols], y[:, t, cols], gcols, ALU.add).then_inc(merged, 1)
            for n in range(4):
                t, s = n % 2, n // 2
                cols = slice(512 * s, 512 * s + 512)
                src = product(dve, f"wo{n}")
                dve.tensor_tensor(resid[:, t, cols], src, resid[:, t, cols], ALU.add).then_inc(emptied["dve"], 1)
            dve.wait_ge(emptied["dve"], ORDINAL["wo3"] + 1)
            dve.memset(stat[:, 61:62], 0.0).then_inc(w_free, RING)
            dve.memset(stat[:, 60:61], 0.0).then_inc(t_read, 1)
            dve.wait_ge(x2_sq, TT)
            mean_eps(slice(20, 22), slice(22, 24), D, x2_ms)
            dve.wait_ge(x2_rt, 1)
            settle(dve.reciprocal(stat[:, 22:24], stat[:, 22:24]))
            dve.wait_ge(late_in, 5 * 16)
            for t in range(TT):
                dve.scalar_tensor_tensor(out=h2[:, t, :], in0=resid[:, t, :], scalar=stat[:, 22 + t:23 + t],
                                         in1=gain_ffn[:, :], op0=ALU.mult, op1=ALU.mult).then_inc(h2_done, 1)
            dve.wait_ge(h2_done, 2)
            for t in range(TT):
                settle(dve.tensor_copy(h2hi[:, t, :], h2[:, t, :]))
                dve.tensor_tensor(h2lo[:, t, :], h2[:, t, :], h2hi[:, t, :].bitcast(F32), ALU.subtract).then_inc(h2_split, 1)
            def low_part(G, i, j, last=False):
                n = nth(i, j, last)
                dve.wait_ge(hi_done, G * (GE * EJ) + n + 1)
                dve.tensor_tensor(low_slot(n), ring_slot(n), high_slot(n).bitcast(F32), ALU.subtract).then_inc(lo_done, 1)

            low_part(0, -1, 6)
            dve.tensor_copy(gatesT[:, :], product(dve, "logitsT")[0:EXPERTS, 0:TOKENS]).then_inc(emptied["dve"], 1)
            src = product(dve, "logits")[:, 0:TT * EXPERTS].rearrange("p (t e) -> p t e", t=TT)
            dve.tensor_tensor(lg[:, :, :], src, brouter[:, :].unsqueeze(1).to_broadcast([P, TT, EXPERTS]), ALU.add).then_inc(emptied["dve"], 1)
            dve.wait_ge(emptied["dve"], ORDINAL["logits"] + 1)
            for t in range(TT):
                settle(dve.max(out=top[:, t, :], in_=lg[:, t, :]))
                settle(dve.max_index(out=topi[:, t, :], in_max=top[:, t, :], in_values=lg[:, t, :]))
                settle(dve.tensor_copy(topf[:, t, :], topi[:, t, :]))
                dve.tensor_scalar(tg[:, t, 4:5], top[:, t, 0:1], -1.0, None, ALU.mult).then_inc(top_done, 1)
            experts = iota_e[:, :].unsqueeze(1).unsqueeze(1).to_broadcast([P, TT, TOPK, EXPERTS])
            settle(dve.tensor_tensor(onehot[:, :, :, :], experts,
                                     topf[:, :, 0:TOPK].unsqueeze(3).to_broadcast([P, TT, TOPK, EXPERTS]), ALU.is_equal))
            settle(dve.tensor_reduce(picked[:, :, :], onehot[:, :, :, :].rearrange("p t k e -> p t e k"), AX.X, ALU.add))
            dve.tensor_copy(pickedb[:, :, :], picked[:, :, :]).then_inc(picked_done, 1)
            src = product(dve, "rank")
            rank = src[:, 0:TT * EXPERTS].rearrange("p (t e) -> p t e", t=TT)
            settle(dve.scalar_tensor_tensor(out=picked[:, :, :], in0=rank, scalar=1.0, in1=picked[:, :, :], op0=ALU.add, op1=ALU.mult))
            dve.tensor_reduce(load[:, 0:1], src[:, TT * EXPERTS:(TT + 1) * EXPERTS], AX.X, ALU.max).then_inc(emptied["dve"], 1)
            slots = slot_no[:, 0:CAP].unsqueeze(1).to_broadcast([P, GE, CAP])
            for b in range(PASSES):
                settle(dve.tensor_scalar(pos[:, :, EXPERTS * b:EXPERTS * b + EXPERTS], picked[:, :, :], -1.0 - CAP * b, None, ALU.add))
                if b == 0:
                    for t in range(TT):
                        ins = dve.tensor_tensor(pick[:, t, :].rearrange("p (i s) -> p i s", i=GE), slots,
                                                pos[:, t, 0:GE].unsqueeze(2).to_broadcast([P, GE, CAP]), ALU.is_equal)
                    ins.then_inc(pick_ready, 1)
                    low_part(0, -1, 7)
            dve.wait_ge(top_exp, 2)
            settle(dve.reciprocal(tg[:, :, 6:7], tg[:, :, 5:6]))
            settle(dve.tensor_tensor(tg[:, :, 0:4], tg[:, :, 0:4], tg[:, :, 6:7].to_broadcast([P, TT, TOPK]), ALU.mult))
            settle(dve.tensor_tensor(onehot[:, :, :, :], onehot[:, :, :, :],
                                     tg[:, :, 0:TOPK].unsqueeze(3).to_broadcast([P, TT, TOPK, EXPERTS]), ALU.mult))
            dve.tensor_reduce(gates[:, :, 0:EXPERTS], onehot[:, :, :, :].rearrange("p t k e -> p t e k"), AX.X,
                              ALU.add).then_inc(gates_done, 1)
            dve.wait_ge(gates_done, 1)
            dve.memset(pos[:, :, PASSES * EXPERTS:], -1.0)
            dve.tensor_copy(gates[:, :, EXPERTS:EXPERTS + GE], gates[:, :, 0:GE])
            dve.wait_ge(emptied["dve"], ORDINAL["rank"] + 1)
            settle(dve.tensor_scalar(load[:, 1:2], load[:, 0:1], float(CAP), float(EXPERTS), ALU.is_gt, ALU.mult))
            settle(dve.tensor_scalar(load[:, 2:3], load[:, 0:1], 2.0 * CAP, float(EXPERTS), ALU.is_gt, ALU.mult))
            settle(dve.tensor_scalar(load[:, 3:4], load[:, 0:1], 3.0 * CAP, float(EXPERTS), ALU.is_gt, ALU.mult))
            settle(dve.tensor_tensor(load[:, 1:2], load[:, 1:2], load[:, 2:3], ALU.add))
            settle(dve.scalar_tensor_tensor(out=load[:, 1:2], in0=load[:, 1:2], scalar=float(EXPERTS), in1=load[:, 3:4], op0=ALU.add, op1=ALU.add))
            dve.tensor_copy(runs_int[:, :], load[:, 1:2]).then_inc(routed, 1)
            dve.tensor_copy(gatesT[:, :], product(dve, "gatesT")[0:EXPERTS, 0:TOKENS]).then_inc(emptied["dve"], 1)
            low_part(0, -1, 9)

            dve.wait_ge(emptied["dve"], ORDINAL["gatesT"] + 1)
            dve.memset(psy[:, :, :], 0.0).then_inc(zeroed, 1)
            dve.wait_ge(routed, 1)
            runs = dve.value_load(runs_int[0:1, 0:1], min_val=0, max_val=PASSES * EXPERTS)

            def glu_begin(G, i, hf, g):
                n = G * (2 * GE) + 2 * i + hf + 1
                dve.wait_ge(t_filled, n)
                bias = bgu[:, bass.ds(g * GE + i, 1), 8 * hf:8 * hf + 8].rearrange("p e c -> p (e c)")
                bias = bias.unsqueeze(2).to_broadcast([P, 8, CAP])
                dve.tensor_tensor(gu[:, :, :], pst[:, :].rearrange("p (c s) -> p c s", c=8),
                                  bias, ALU.add).then_inc(t_read, 1)
                dve.wait_ge(t_read, n + 1)
                dve.tensor_scalar(gu[:, 0:4, :], gu[:, 0:4, :], LIMIT, None, ALU.min).then_inc(glu_done, 1)
                dve.tensor_scalar(lin[:, :, :], gu[:, 4:8, :], LIMIT, -LIMIT, ALU.min, ALU.max).then_inc(lin_done, 1)

            def glu_end(G, i, hf):
                n = G * (2 * GE) + 2 * i + hf + 1
                dve.wait_ge(lin_done, n)
                dve.scalar_tensor_tensor(out=lin[:, :, :], in0=lin[:, :, :], scalar=1.0, in1=gu[:, 0:4, :],
                                         op0=ALU.add, op1=ALU.mult).then_inc(prod_done, 1)
                dve.wait_ge(prod_done, n)
                dve.wait_ge(sig_done, n)
                dve.tensor_tensor(af[:, :, :], lin[:, :, :], sg[:, :, :], ALU.mult).then_inc(af_done, 1)
                dve.wait_ge(af_done, n)
                ks = slice(4 * hf, 4 * hf + 4)
                dve.tensor_copy(actT[:, ks, 0:CAP], af[:, :, :]).then_inc(ahi_done, 1)
                dve.wait_ge(ahi_done, n)
                dve.tensor_tensor(actT[:, ks, CAP:P], af[:, :, :], actT[:, ks, 0:CAP].bitcast(F32),
                                  ALU.subtract).then_inc(act_ready, 1)

            def add_scattered(before, p, last=False):
                t, s = p // 2, p % 2
                cols = slice(512 * s, 512 * s + 512)
                dve.wait_ge(sc_filled, before + 1)
                dve.tensor_tensor(resid[:, t, cols], sc_bank(p, last), resid[:, t, cols], ALU.add).then_inc(y_added, 1)

            def turn(G, i, g, last=False):
                E = G * GE + i
                for j in range(EJ):
                    if last and 6 <= j < 10:
                        continue
                    if j in DVE_PLACES:
                        low_part(G, i, j, last and j >= 10)
                    if j == 4:
                        glu_begin(G, i, 0, g)
                    if j == 5:
                        glu_end(G, i, 0)
                    if i % 2 == 0 and j in (6, 9):
                        for p in ((0, 1, 2) if j == 6 else (3,)):
                            add_scattered(E * 2 + p, p)
                    if j == (10 if last else 9):
                        glu_begin(G, i, 1, g)
                    if j == (11 if last else 10):
                        glu_end(G, i, 1)

            with dve.Fori(0, PASSES) as b:
                with dve.If(runs > b * EXPERTS):
                    with dve.Fori(0, NG) as g:
                        G = b * NG + g
                        for i in range(GE - 1):
                            turn(G, i, g)
                        with dve.If(runs > G * GE + GE):
                            turn(G, GE - 1, g)
                        with dve.Else():
                            turn(G, GE - 1, g, last=True)
            for p in range(4):
                add_scattered(runs * 2 + p, p, last=True)

        @block.tensor
        def _(pe):
            def begin(name):
                n = INDEX[name]
                if n >= 8:
                    before, who = PRODUCTS[n - 8]
                    pe.wait_ge(emptied[who], ORDINAL[before] + 1)
                return bank(name)

            def landed(n):
                pe.wait_ge(raw_in[n % RAW], raw_in_count(n))

            pe.wait_ge(consts, 1)
            for n in range(4):
                t, h = n % 2, n // 2
                pe.wait_ge(xn_done, t + 1)
                o = begin(f"hT{n}")
                for k in range(4):
                    kk = 4 * h + k
                    ins = pe.transpose(o[:, P * k:P * k + P], xn[:, t, P * kk:P * kk + P], ident[:, :])
                ins.then_inc(filled, 1)
            pe.wait_ge(emptied["dve"], ORDINAL["hT3"] + 1)

            def tokens_product(name, src, t, slots, c0, width):
                o = begin(name)
                total = sum(FRONT_SLOTS[s][2] for s in slots)
                k = 0
                for s in slots:
                    landed(s)
                    for kk in range(FRONT_SLOTS[s][2]):
                        ins = pe.matmul(o[:, 0:width], src[:, k, P * t:P * t + P],
                                        front_slot(s)[:, kk, c0:c0 + width], start=(k == 0), stop=(k == total - 1))
                        k += 1
                ins.then_inc(filled, 1)
                return ins

            slot = 0
            for part, width in ((0, CA), (1, CB_)):
                for t in range(TT):
                    tokens_product(f"lat{2 * part + t}", hT, t, (slot, slot + 1), 0, width)
                slot += 2
            for s in range(3):
                for half in range(2):
                    n = 2 * s + half
                    o = begin(f"xbc{n}")
                    for c in range(2):
                        for k in range(KD):
                            sl = slot + k // 4
                            if c == 0:
                                landed(sl)
                            cc = P * (2 * half + c)
                            ins = pe.matmul(o[:, TOKENS * c:TOKENS * c + TOKENS], front_slot(sl)[:, k % 4, cc:cc + P],
                                            hT[:, k, :], start=(k == 0), stop=(k == KD - 1))
                    ins.then_inc(filled, 1)
                slot += 2
            for s in range(2):
                for t in range(TT):
                    tokens_product(f"z{2 * s + t}", hT, t, (slot, slot + 1), 0, 512)
                slot += 2
            pe.wait_ge(lat_done, 2 * TT)
            for n in range(4):
                t, part = n % 2, n // 2
                c0, kk = (HEADS, 3) if part == 0 else (CA, 2)
                o = begin(f"latT{n}")
                for k in range(kk):
                    ins = pe.transpose(o[:, P * k:P * k + P], lat[:, t, c0 + P * k:c0 + P * k + P], ident[:, :])
                ins.then_inc(filled, 1)
            pe.wait_ge(emptied["dve"], ORDINAL["latT3"] + 1)
            for s in range(3):
                for t in range(TT):
                    tokens_product(f"qup{2 * s + t}", latent_T[:, 0:3], t, (slot,), 0, 512)
                slot += 1
            for s in range(4):
                for t in range(TT):
                    tokens_product(f"kvup{2 * s + t}", latent_T[:, 3:5], t, (slot,), 512 * (s % 2), 512)
                if s % 2:
                    slot += 1
            def gate_products(s, slot):
                for t in range(TT):
                    tokens_product(f"gate{2 * s + t}", hT, t, (slot, slot + 1), 0, 512)

            for s in range(3):
                gate_products(s, slot)
                slot += 2
            pe.wait_ge(silu_done, 3)
            for n in range(4):
                t, h = n % 2, n // 2
                o = begin(f"xsT{n}")
                for k in range(4):
                    ins = pe.transpose(o[:, P * k:P * k + P], xc[:, 4 * h + k, P * t:P * t + P], ident[:, :])
                ins.then_inc(filled, 1)
            o = begin("btok")
            for g in range(GROUPS):
                ins = pe.transpose(o[:, P * g:P * g + P], xc[:, KD + g, 0:P], ident[:, :])
            ins.then_inc(filled, 1)
            o = begin("cb")
            for t in range(TT):
                for g in range(GROUPS):
                    a = P * (2 * t + g)
                    ins = pe.matmul(o[:, a:a + P], xc[:, KD + g, P * t:P * t + P], xc[:, KD + GROUPS + g, P * t:P * t + P],
                                    start=True, stop=True)
            ins.then_inc(filled, 1)
            pe.wait_ge(dt_done, 1)
            o = begin("acum")
            for t in range(TT):
                pe.matmul(o[:, HEADS * t:HEADS * t + HEADS], upper[:, :], sp[:, 5, t, :], start=True, stop=True)
            pe.matmul(o[:, 2 * HEADS:3 * HEADS], ones[:, :], sp[:, 5, 0, :], start=True, stop=True).then_inc(filled, 1)

            def cumulated(n):
                t = n // 4
                o = begin(f"acumb{n}")
                for hh in range(4):
                    h = 4 * (n % 4) + hh
                    v = o[:, P * hh:P * hh + P]
                    pe.matmul(v, sp[:, 5, t, h:h + 1].to_broadcast([P, P]), upper[:, :], start=True, stop=False)
                    ins = pe.matmul(v, identb[:, :], causal[:, :], start=False, stop=True)
                ins.then_inc(filled, 1)

            def state(g):
                o = begin(f"state{g}")
                pe.matmul(o, btok[:, P * g:P * g + P], xdec[:, 512 * g:512 * g + 512], start=True, stop=True).then_inc(filled, 1)

            def from_state(g):
                o = begin(f"yoff{g}")
                pe.matmul(o, xc[:, KD + GROUPS + g, P:2 * P], prev[:, 512 * g:512 * g + 512], start=True, stop=True).then_inc(filled, 1)

            def ssd_out(n):
                t, g = n // 2, n % 2
                o = begin(f"ydiag{n}")
                for half in range(2):
                    m = 2 * n + half
                    pe.wait_ge(mmat_done, m + 1)
                    for hh in range(4):
                        c = HD * (4 * half + hh)
                        ins = pe.matmul(o[:, c:c + HD], lmat[:, m % 4, hh, :], xdt[:, t, 512 * g + c:512 * g + c + HD],
                                        start=True, stop=True)
                ins.then_inc(filled, 1)

            for n in range(4):
                cumulated(n)
            pe.wait_ge(xdt_done, 1)
            for g in range(GROUPS):
                state(g)
            pe.wait_ge(emptied["dve"], ORDINAL["state1"] + 1)
            for g in range(GROUPS):
                from_state(g)
            ssd_out(0)
            cumulated(4)
            cumulated(5)
            ssd_out(1)
            cumulated(6)
            cumulated(7)
            ssd_out(2)
            ssd_out(3)
            pe.wait_ge(q_done, TT)
            for n in range(6):
                t, part = n % 2, n // 2
                o = begin(f"qT{n}")
                for k in range(4):
                    src = qb[:, t, 4 * part + k, 0:NOPE] if part < 2 else qr[:, t, P * k:P * k + P]
                    ins = pe.transpose(o[:, P * k:P * k + P], src, ident[:, :])
                ins.then_inc(filled, 1)
            pe.wait_ge(k_done, TT)
            for n in range(6):
                t, part = n % 2, n // 2
                o = begin(f"kT{n}")
                for k in range(4):
                    src = kv[:, t, 4 * part + k, 0:NOPE] if part < 2 else kr[:, t, 2 * k:2 * k + 2, :].rearrange("p h n -> p (h n)")
                    ins = pe.transpose(o[:, P * k:P * k + P], src, ident[:, :])
                ins.then_inc(filled, 1)
            gate_products(3, slot)
            slot += 2
            pe.wait_ge(yn_done, 4)
            for n in range(4):
                t, h = n % 2, n // 2
                o = begin(f"yT{n}")
                for k in range(4):
                    kk = 4 * h + k
                    ins = pe.transpose(o[:, P * k:P * k + P], y[:, t, P * kk:P * kk + P], ident[:, :])
                ins.then_inc(filled, 1)
            pe.wait_ge(emptied["dve"], ORDINAL["yT3"] + 1)
            ssd_slot = slot
            slot += 4

            def ssd_projection(n):
                a = ssd_slot + 2 * (n // 2)
                tokens_product(f"ssdout{n}", yT, n % 2, (a, a + 1), 0, 512)

            pe.wait_ge(emptied["act"], ORDINAL["kT5"] + 1)

            def scores(n):
                j, h0, hs = SCORES[n]
                keys = P * (j + 1)
                o = begin(f"S{n}")
                qs = slice(P * j, P * j + P)
                for hh in range(hs):
                    h = h0 + 2 * hh
                    a = keys * hh
                    half = slice(64 * (h % 2), 64 * (h % 2) + 64)
                    pe.matmul(o[:, a:a + keys], qT[:, h, qs], kT[:, h, 0:keys], start=True, stop=False)
                    pe.matmul(o[:, a:a + keys], qrT[half, h // 2, qs], krT[half, h // 2, 0:keys], start=False, stop=False)
                    ins = pe.matmul(o[:, a:a + keys], identb[:, :], amask[:, 2 * P - keys:2 * P], start=False, stop=True)
                ins.then_inc(filled, 1)

            def turn_probs(n):
                j, _, hs = SCORES[n]
                pe.wait_ge(prob_done, n + 1)
                o = begin(f"PT{n}")
                for k in range(4):
                    ins = pe.transpose(o[:, P * k:P * k + P], prob[:, n % 3, P * k:P * k + P], ident[:, :])
                ins.then_inc(filled, 1)

            def values(n):
                j, h0, hs = SCORES[n]
                pe.wait_ge(emptied["act"], ORDINAL[f"PT{n}"] + 1)
                o = begin(f"O{n}")
                for hh in range(hs):
                    for kt in range(j + 1):
                        a = P * ((j + 1) * hh + kt)
                        ins = pe.matmul(o[:, P * hh:P * hh + P], kv[:, kt, h0 + 2 * hh, NOPE:NOPE + VD],
                                        probT[:, n % 3, a:a + P], start=(kt == 0), stop=(kt == j))
                ins.then_inc(filled, 1)

            for name, _ in PRODUCTS[INDEX["S0"]:INDEX["O5"] + 1]:
                {"S": scores, "P": turn_probs, "O": values, "s": ssd_projection}[name[0]](int(name[-1]))
            pe.wait_ge(emptied["dve"], ORDINAL["O5"] + 1)
            for s in range(2):
                for t in range(TT):
                    tokens_product(f"mlaout{2 * s + t}", oT, t, (slot, slot + 1), 0, 512)
                slot += 2
            for n in range(4):
                t, h = n % 2, n // 2
                pe.wait_ge(merged, n + 1)
                o = begin(f"mT{n}")
                for k in range(4):
                    kk = 4 * h + k
                    ins = pe.transpose(o[:, P * k:P * k + P], y[:, t, P * kk:P * kk + P], ident[:, :])
                ins.then_inc(filled, 1)
            pe.wait_ge(emptied["act"], ORDINAL["mT3"] + 1)
            for s in range(2):
                for t in range(TT):
                    tokens_product(f"wo{2 * s + t}", mT, t, (slot, slot + 1), 0, 512)
                slot += 2
            assert slot == NF
            for n in range(4):
                t, h = n % 2, n // 2
                pe.wait_ge(h2_done, t + 1)
                o = begin(f"h2T{n}")
                for k in range(4):
                    kk = 4 * h + k
                    ins = pe.transpose(o[:, P * k:P * k + P], h2[:, t, P * kk:P * kk + P], ident[:, :])
                ins.then_inc(filled, 1)
            pe.wait_ge(emptied["act"], ORDINAL["h2T3"] + 1)
            pe.wait_ge(late_in, 5 * 16)
            o = begin("logitsT")
            for k in range(KD):
                ins = pe.matmul(o[0:EXPERTS, 0:TOKENS], wrouter[:, k, :], h2T[:, k, :], start=(k == 0), stop=(k == KD - 1))
            ins.then_inc(filled, 1)
            pe.wait_ge(emptied["dve"], ORDINAL["logitsT"] + 1)
            o = begin("logits")
            for t in range(TT):
                ins = pe.transpose(o[:, EXPERTS * t:EXPERTS * t + EXPERTS], gatesT[:, P * t:P * t + P],
                                   ident[0:EXPERTS, 0:EXPERTS])
            ins.then_inc(filled, 1)
            pe.wait_ge(picked_done, 1)
            o = begin("rank")
            pe.matmul(o[:, 0:EXPERTS], strictb[:, :], pickedb[:, 0, :], start=True, stop=True)
            pe.matmul(o[:, EXPERTS:2 * EXPERTS], onesb[:, :], pickedb[:, 0, :], start=True, stop=False)
            pe.matmul(o[:, EXPERTS:2 * EXPERTS], strictb[:, :], pickedb[:, 1, :], start=False, stop=True)
            pe.matmul(o[:, 2 * EXPERTS:3 * EXPERTS], onesb[:, :], pickedb[:, 0, :], start=True, stop=False)
            pe.matmul(o[:, 2 * EXPERTS:3 * EXPERTS], onesb[:, :], pickedb[:, 1, :], start=False, stop=True).then_inc(filled, 1)
            def gather(k, to=psm):
                for part, src in enumerate((h2hi, h2lo)):
                    for t in range(TT):
                        ins = pe.matmul(to[:, 256 * part:256 * part + 256], src[:, t, P * k:P * k + P], pick[:, t, :],
                                        start=(t == 0), stop=(t == TT - 1))
                ins.then_inc(x_filled, 1)

            def split_landed(G, i, j, last=False):
                if j in POOL_PLACES:
                    pe.wait_ge(lo_done_pool, low_order(POOL_PLACES, POOL_FIRST, G, i, j))
                else:
                    pe.wait_ge(lo_done, low_order(DVE_PLACES, 0 if last else DVE_FIRST, G, i, j))

            def gate_up_chunk(i, n, k, hf):
                for part, w in enumerate((high_slot(n), low_slot(n))):
                    for s in range(2):
                        o = ps[s][:, :] if hf == 0 else ps2[:, s, :]
                        a = D * (k % 2) + 512 * s
                        ins = pe.matmul(o, xT[:, k, i, :], w[:, a:a + 512],
                                        start=(k == 0 and part == 0), stop=(k == KD - 1 and part == 1))
                return ins

            def first_half_slot(G, i, j):
                split_landed(G, i, j)
                for k in (2 * (j - 6), 2 * (j - 6) + 1):
                    if i in (-1, GE - 1):
                        pe.wait_ge(x_out, (G + (i > 0)) * KD + k + 1)
                    ins = gate_up_chunk((i + 1) % GE, nth(i, j), k, 0)
                    if i < 0 and k < KD - 2:
                        gather(k + 2, (psm, pst)[k % 2])
                ins.then_inc(w_free, 1)

            def down_slot(G, i, j, last=False):
                split_landed(G, i, j, last)
                n = nth(i, j, last)
                for k2 in range(2):
                    k = 2 * (j - 4 if j < 6 else j - 8) + k2
                    for part, w in enumerate((high_slot(n), low_slot(n))):
                        for s in range(2):
                            a = D * k2 + 512 * s
                            ins = pe.matmul(psy[:, s, :], actT[:, k, :], w[:, a:a + 512],
                                            start=(k == 0 and part == 0), stop=(k == KD - 1 and part == 1))
                ins.then_inc(w_free, 1)

            def turn_sums(G, i, hf):
                pe.wait_ge(gu_out, G * (4 * GE) + 4 * i + 2 * hf + 2)
                pe.wait_ge(t_read, G * (2 * GE) + 2 * i + hf + 1)
                for c in range(8):
                    ins = pe.matmul(pst[:, CAP * c:CAP * c + CAP], gusb[:, hf, P * c:P * c + P], stacked[:, :],
                                    start=True, stop=True)
                ins.then_inc(t_filled, 1)

            def turn_gates(E, i):
                pe.wait_ge(give_ready, E + 1)
                for t in range(TT):
                    ins = pe.transpose(psm[:, P * t:P * t + P], give[:, i, t, :], ident[:, :])
                ins.then_inc(g_filled, 1)

            def scatter(p, first):
                t, s = p // 2, p % 2
                for m in range(2):
                    ins = pe.matmul(sc_bank(p), giveT[:, (first + m) % GE, P * t:P * t + P],
                                    ysb[:, m, 512 * s:512 * s + 512], start=(m == 0), stop=(m == 1))
                ins.then_inc(sc_filled, 1)

            def scatter_last(p, m):
                t, s = p // 2, p % 2
                cols = slice(512 * s, 512 * s + 512)
                if m == 0:
                    pe.matmul(sc_bank(p, last=True), gatesT[:, P * t:P * t + P], bdown[:, cols], start=True, stop=False)
                ins = pe.matmul(sc_bank(p, last=True), giveT[:, GE - 2 + m, P * t:P * t + P], ysb[:, m, cols],
                                start=False, stop=(m == 1))
                if m == 1:
                    ins.then_inc(sc_filled, 1)

            pe.wait_ge(h2_split, 2)
            pe.wait_ge(pick_ready, 1)
            gather(0, psm)
            gather(1, pst)
            for j in range(6, 10):
                if j == 8:
                    pe.wait_ge(gates_done, 1)
                    o = begin("gatesT")
                    for t in range(TT):
                        ins = pe.transpose(o[0:EXPERTS, P * t:P * t + P], gates[:, t, 0:EXPERTS], ident[:, :])
                    ins.then_inc(filled, 1)
                first_half_slot(0, -1, j)
            pe.wait_ge(emptied["dve"], ORDINAL["gatesT"] + 1)
            pe.wait_ge(x_out, KD)
            runs = pe.value_load(runs_int[0:1, 0:1], min_val=0, max_val=PASSES * EXPERTS)

            def turn(G, i, last=False):
                E = G * GE + i
                if i % 2:
                    pe.wait_ge(y_added, 2 * E + 2)
                turn_gates(E, i)
                for j in range(4):
                    split_landed(G, i, j)
                    for k in (2 * j, 2 * j + 1):
                        ins = gate_up_chunk(i, nth(i, j), k, 1)
                        if k % 2:
                            ins.then_inc(w_free, 1)
                        if i == GE - 1 and not last:
                            if k == 0:
                                pe.wait_ge(pick_ready, G + 2)
                                pe.wait_ge(g_out, E + 1)
                            else:
                                pe.wait_ge(x_out, G * KD + KD + k)
                            gather(k)
                    if j == 1:
                        turn_sums(G, i, 0)
                pe.wait_ge(y_out, E + 1)
                if i % 2 == 0:
                    pe.wait_ge(g_out, E + 1)
                    for p in range(3):
                        scatter(p, i - 2)
                pe.wait_ge(act_ready, G * (2 * GE) + 2 * i + 1)
                down_slot(G, i, 4)
                if last:
                    turn_sums(G, i, 1)
                down_slot(G, i, 5)
                if last:
                    pe.wait_ge(g_out, E + 1)
                    for p in range(3):
                        scatter_last(p, 0)
                    pe.wait_ge(t_read, 2 * E + 3)
                    scatter_last(3, 0)
                else:
                    pe.wait_ge(y_added, 2 * E + 2)
                    first_half_slot(G, i, 6)
                    turn_sums(G, i, 1)
                    if i % 2 == 0:
                        pe.wait_ge(y_added, 2 * E + 3)
                        scatter(3, i - 2)
                    for j in (7, 8, 9):
                        first_half_slot(G, i, j)
                pe.wait_ge(act_ready, G * (2 * GE) + 2 * i + 2)
                for j in (10, 11):
                    down_slot(G, i, j, last)

            with pe.Fori(0, PASSES) as b:
                with pe.If(runs > b * EXPERTS):
                    with pe.Fori(0, NG) as g:
                        G = b * NG + g
                        for i in range(GE - 1):
                            turn(G, i)
                        with pe.If(runs > G * GE + GE):
                            turn(G, GE - 1)
                        with pe.Else():
                            turn(G, GE - 1, last=True)
            pe.wait_ge(y_out, runs + 1)
            for p in range(4):
                scatter_last(p, 1)


def kernel(x, g_mix, w_in, conv_w, conv_b, dt_bias, a_log, d_skip, g_ssd_out, w_ssd_out, g_q_lat, w_q_up,
           g_kv_lat, w_kv_up, g_qk_q, g_qk_k, w_mla_out, w_o, g_ffn, w_router, b_router, w_gate_up,
           b_gate_up, w_down, b_down):
    import concourse.bacc as bacc
    from concourse.bass_utils import run_bass_kernel_spmd

    def columns(v, n):
        return np.asarray(v).reshape(n, P).T

    def rows(v):
        v = np.asarray(v).reshape(1, -1)
        return np.repeat(v, P, axis=0)

    pos = np.arange(TOKENS, dtype=np.float32)
    inv = (np.float32(10000.0) ** (-np.arange(0, ROPE, 2, dtype=np.float32) / np.float32(ROPE))).astype(np.float32)
    ang = (pos[:, None] * inv[None, :]).astype(np.float32)

    def table(a):
        return a.astype(np.float32).reshape(TT, P, ROPE // 2).transpose(1, 0, 2)

    host = {
        "x": np.asarray(x)[0],
        "w_in": np.asarray(w_in)[0], "w_q_up": np.asarray(w_q_up)[0], "w_kv_up": np.asarray(w_kv_up)[0],
        "w_ssd_out": np.asarray(w_ssd_out)[0], "w_mla_out": np.asarray(w_mla_out)[0], "w_o": np.asarray(w_o)[0],
        "w_router": np.asarray(w_router)[0].reshape(KD, P, EXPERTS).transpose(1, 0, 2),
        "w_gate_up": np.asarray(w_gate_up)[0].reshape(EXPERTS, 4, 2, P, 2, 2, 512).transpose(0, 5, 1, 3, 2, 4, 6)
        .reshape(EXPERTS, 8, P, SLOT),
        "w_down": np.asarray(w_down)[0].reshape(EXPERTS, 4, 2, P, D).transpose(0, 1, 3, 2, 4).reshape(EXPERTS, 4, P, SLOT),
        "g_mix": columns(g_mix, KD), "conv_w": np.asarray(conv_w)[0].reshape(CONV, XC, P).transpose(2, 1, 0),
        "conv_b": columns(conv_b, XC), "dt_bias": rows(dt_bias), "a_log": rows(a_log), "d_skip": rows(d_skip),
        "g_ssd_out": columns(g_ssd_out, KD), "g_q_lat": columns(g_q_lat, 3), "g_kv_lat": columns(g_kv_lat, 2),
        "g_qk_q": rows(g_qk_q), "g_qk_k": rows(g_qk_k), "g_ffn": rows(g_ffn), "b_router": rows(b_router),
        "b_gate_up": np.asarray(b_gate_up)[0].reshape(EXPERTS, 2, 2, 4, P).transpose(4, 0, 2, 1, 3).reshape(P, EXPERTS, 16),
        "b_down": np.asarray(b_down)[0],
        "cos": table(np.cos(ang)), "sin": table(np.sin(ang)),
    }
    nc = bacc.Bacc("TRN2", target_bir_lowering=False, num_devices=1)
    arrays, args = {}, {}
    for name, a in host.items():
        a = np.ascontiguousarray(a)
        arrays[f"in_{name}"] = a
        args[name] = nc.dram_tensor(f"in_{name}", a.shape, mybir.dt.from_np(a.dtype), kind="ExternalInput").ap()
    out = nc.dram_tensor("out_x", (TOKENS, D), F32, kind="ExternalOutput").ap()
    build(nc, out=out, **args)
    r = run_bass_kernel_spmd(nc, [arrays], core_ids=[0])
    return r.results[0]["out_x"].reshape(1, TOKENS, D)
```
